# Optimizing a Trainium2 kernel written in Bass

```python
import jax, jax.numpy as jnp
from jax import lax
import numpy as np

D_MODEL = 1024
BATCH = 1
SEQ = 512
DEPTH = 2

ATT_HEAD_DIM = 64
ATT_DIM = D_MODEL // 2
ATT_HEADS = ATT_DIM // ATT_HEAD_DIM
Q_BLOCK = 128
CONV_DIM = D_MODEL // 2
CONV_WIDTH = 3
POOL_WINDOWS = (2, 4, 8, 16)
N_POOL_GROUPS = len(POOL_WINDOWS)
POOL_DIM = D_MODEL // 2
POOL_GROUP_DIM = POOL_DIM // N_POOL_GROUPS
N_BRANCHES = 3
BRANCH_DIM = D_MODEL // 2
IN_COLS = 3 * ATT_DIM + 3 * CONV_DIM + POOL_DIM + N_BRANCHES * D_MODEL
PEER_HEADS = 8
N_KEYS = 128
N_EXPERTS = N_KEYS * N_KEYS
PEER_QUERY_DIM = 256
PEER_HALF_DIM = PEER_QUERY_DIM // 2
PEER_TOPK = 16
PEER_TOKEN_CHUNK = 128
PLE_DIM = 256
RMS_EPS = 1e-6

kernel_name = "hybrid_stickbreak_conv_pool_peer"

def rmsnorm(x, g):
    xf = x.astype(jnp.float32)
    y = xf * lax.rsqrt(jnp.mean(xf * xf, axis=-1, keepdims=True) + RMS_EPS)
    return (y * g.astype(jnp.float32)).astype(x.dtype)

def stick_breaking_attention(q, k, v):
    b, h, s, dh = q.shape
    nb = s // Q_BLOCK
    scale = dh ** -0.5
    q_blocks = q.reshape(b, h, nb, Q_BLOCK, dh).transpose(2, 0, 1, 3, 4)
    k_pos = jnp.arange(s)

    def block(args):
        blk, q_blk = args
        q_pos = blk * Q_BLOCK + jnp.arange(Q_BLOCK)
        mask = k_pos[None, :] < q_pos[:, None]
        z = jnp.einsum('bhqd,bhkd->bhqk', q_blk, k).astype(jnp.float32) * scale
        log_beta = jax.nn.log_sigmoid(z)
        log_stay = jnp.where(mask, jax.nn.log_sigmoid(-z), 0.0)
        log_remain = lax.cumsum(log_stay, axis=3, reverse=True) - log_stay
        w = jnp.where(mask, jnp.exp(log_beta + log_remain), 0.0)
        return jnp.einsum('bhqk,bhkd->bhqd', w.astype(v.dtype), v)

    out = lax.map(block, (jnp.arange(nb), q_blocks))
    return out.transpose(1, 2, 0, 3, 4).reshape(b, h, s, dh)

def causal_short_conv(u, w):
    s = u.shape[1]
    up = jnp.pad(u, ((0, 0), (CONV_WIDTH - 1, 0), (0, 0)))
    return sum(w[j] * up[:, j:j + s] for j in range(CONV_WIDTH))

def causal_pool_mixer(u, pool_w):
    s = u.shape[1]
    pos = jnp.arange(s)
    outs = []
    for gi, win in enumerate(POOL_WINDOWS):
        ug = u[..., gi * POOL_GROUP_DIM:(gi + 1) * POOL_GROUP_DIM].astype(jnp.float32)
        cs = jnp.cumsum(ug, axis=1)
        shifted = jnp.pad(cs, ((0, 0), (win, 0), (0, 0)))[:, :s]
        count = jnp.minimum(pos + 1, win).astype(jnp.float32)
        pooled = (cs - shifted) / count[None, :, None] - ug
        outs.append(jnp.einsum('bsc,cd->bsd', pooled.astype(u.dtype), pool_w[gi]))
    return jnp.concatenate(outs, axis=-1)

def peer_ffn(xn, w_query, sub_keys, expert_u, expert_v):
    b, s, d = xn.shape
    q = jnp.einsum('bsd,dn->bsn', xn, w_query).reshape(b, s, PEER_HEADS, 2, PEER_HALF_DIM)
    scores = jnp.einsum('bshpc,hpkc->bshpk', q, sub_keys).astype(jnp.float32)
    half_vals, half_idx = lax.top_k(scores, PEER_TOPK)
    cand_vals = (half_vals[..., 0, :, None] + half_vals[..., 1, None, :]).reshape(
        b, s, PEER_HEADS, PEER_TOPK * PEER_TOPK)
    cand_idx = (half_idx[..., 0, :, None] * N_KEYS + half_idx[..., 1, None, :]).reshape(
        b, s, PEER_HEADS, PEER_TOPK * PEER_TOPK)
    top_vals, top_pos = lax.top_k(cand_vals, PEER_TOPK)
    expert_idx = jnp.take_along_axis(cand_idx, top_pos, axis=-1)
    gates = jax.nn.softmax(top_vals, axis=-1)

    n_chunks = (b * s) // PEER_TOKEN_CHUNK
    n_sel = PEER_HEADS * PEER_TOPK
    xc = xn.reshape(n_chunks, PEER_TOKEN_CHUNK, d)
    ic = expert_idx.reshape(n_chunks, PEER_TOKEN_CHUNK, n_sel)
    gc = gates.reshape(n_chunks, PEER_TOKEN_CHUNK, n_sel).astype(xn.dtype)

    def chunk(args):
        x_t, i_t, g_t = args
        u = jnp.take(expert_u, i_t, axis=0)
        act = jax.nn.gelu(jnp.einsum('ted,td->te', u, x_t)) * g_t
        return jnp.einsum('te,ted->td', act, jnp.take(expert_v, i_t, axis=0))

    return lax.map(chunk, (xc, ic, gc)).reshape(b, s, d)

def setup_inputs(seed: int = 0) -> dict:
    key = jax.random.key(seed)
    ks = jax.random.split(key, 20)

    def nrm(k, shape, scale):
        return jax.random.normal(k, shape, jnp.float32) * scale

    return {
        "x": nrm(ks[0], (BATCH, SEQ, D_MODEL), 1.0),
        "p": nrm(ks[1], (DEPTH, BATCH, SEQ, PLE_DIM), 1.0),
        "norm_mix": 1.0 + nrm(ks[2], (DEPTH, D_MODEL), 0.02),
        "w_in": nrm(ks[3], (DEPTH, D_MODEL, IN_COLS), D_MODEL ** -0.5),
        "q_norm": 1.0 + nrm(ks[4], (DEPTH, ATT_HEAD_DIM), 0.02),
        "k_norm": 1.0 + nrm(ks[5], (DEPTH, ATT_HEAD_DIM), 0.02),
        "conv_w": nrm(ks[6], (DEPTH, CONV_WIDTH, CONV_DIM), CONV_WIDTH ** -0.5),
        "pool_w": nrm(ks[7], (DEPTH, N_POOL_GROUPS, POOL_GROUP_DIM, POOL_GROUP_DIM), POOL_GROUP_DIM ** -0.5),
        "pool_scale": 1.0 + nrm(ks[8], (DEPTH, POOL_DIM), 0.02),
        "w_branch": nrm(ks[9], (DEPTH, N_BRANCHES, BRANCH_DIM, D_MODEL), BRANCH_DIM ** -0.5),
        "w_out": nrm(ks[10], (DEPTH, D_MODEL, D_MODEL), D_MODEL ** -0.5),
        "norm_ffn": 1.0 + nrm(ks[11], (DEPTH, D_MODEL), 0.02),
        "w_query": nrm(ks[12], (DEPTH, D_MODEL, PEER_HEADS * PEER_QUERY_DIM), D_MODEL ** -0.5),
        "sub_keys": nrm(ks[13], (DEPTH, PEER_HEADS, 2, N_KEYS, PEER_HALF_DIM), PEER_HALF_DIM ** -0.5),
        "expert_u": nrm(ks[14], (DEPTH, N_EXPERTS, D_MODEL), D_MODEL ** -0.5),
        "expert_v": nrm(ks[15], (DEPTH, N_EXPERTS, D_MODEL), PEER_HEADS ** -0.5),
        "norm_ple": 1.0 + nrm(ks[16], (DEPTH, D_MODEL), 0.02),
        "w_ple_gate": nrm(ks[17], (DEPTH, D_MODEL, D_MODEL), D_MODEL ** -0.5),
        "w_ple_proj": nrm(ks[18], (DEPTH, PLE_DIM, D_MODEL), PLE_DIM ** -0.5),
    }

def reference(x, p, norm_mix, w_in, q_norm, k_norm, conv_w, pool_w, pool_scale, w_branch,
              w_out, norm_ffn, w_query, sub_keys, expert_u, expert_v, norm_ple,
              w_ple_gate, w_ple_proj):
    b, s, _ = x.shape
    splits = np.cumsum([ATT_DIM, ATT_DIM, ATT_DIM, CONV_DIM, CONV_DIM, CONV_DIM, POOL_DIM])
    h = x
    for i in range(DEPTH):
        xn = rmsnorm(h, norm_mix[i])
        proj = jnp.einsum('bsd,dn->bsn', xn, w_in[i])
        q, k, v, cb, cc, cu, pu, gate_logits = jnp.split(proj, splits, axis=-1)

        def heads(t):
            return t.reshape(b, s, ATT_HEADS, ATT_HEAD_DIM).transpose(0, 2, 1, 3)
        qh = rmsnorm(heads(q), q_norm[i])
        kh = rmsnorm(heads(k), k_norm[i])
        att = stick_breaking_attention(qh, kh, heads(v))
        att = att.transpose(0, 2, 1, 3).reshape(b, s, ATT_DIM)

        conv = cb * causal_short_conv(cc * cu, conv_w[i])

        pool = causal_pool_mixer(pu, pool_w[i]) * pool_scale[i]

        branches = jnp.stack([att, conv, pool], axis=2)
        branch_d = jnp.einsum('bsjc,jcd->bsjd', branches, w_branch[i])
        gates = jax.nn.sigmoid(gate_logits.reshape(b, s, N_BRANCHES, D_MODEL))
        mixed = jnp.sum(gates * branch_d, axis=2)
        h = h + jnp.einsum('bsd,de->bse', mixed, w_out[i])

        h = h + peer_ffn(rmsnorm(h, norm_ffn[i]), w_query[i], sub_keys[i], expert_u[i], expert_v[i])

        ple_gate = jax.nn.sigmoid(jnp.einsum('bsd,de->bse', rmsnorm(h, norm_ple[i]), w_ple_gate[i]))
        h = h + ple_gate * jnp.einsum('bsr,rd->bsd', p[i], w_ple_proj[i])
    return h


_drawn_inputs = setup_inputs


def setup_inputs(seed=0):
    import zlib

    import numpy as np

    out = dict(_drawn_inputs(seed))
    spreads = {}
    factors = {'q_norm': 4.365, 'k_norm': 4.07, 'pool_scale': 2.696, 'norm_ple': 32.829}
    for name, (base, spread) in spreads.items():
        noise = np.random.default_rng([zlib.crc32(name.encode()), seed]).standard_normal(out[name].shape)
        drawn = base * np.exp(spread * noise) if base else spread * noise
        out[name] = __import__('jax').numpy.asarray(drawn.astype(out[name].dtype))
    for name, factor in factors.items():
        out[name] = (out[name] * factor).astype(out[name].dtype)
    return out
```

```python
import concourse.bass as bass
from concourse import mybir
from contextlib import ExitStack, contextmanager

P = 128
D, SEQ, DEPTH = 1024, 512, 2
DC = D // P
DH, SCALE_ROOT = 64, 8.0
NBLK = SEQ // P
PAIRS = 4
GROUPS = 4
NB = 3
HP, NK, TOPK = 16, 128, 16
PH = HP // 2
SLOTS = PH * TOPK
EPS = 1e-6

RING, RAW, AHEAD = 8, 4, 4
EG = 4
NG = NK // EG
N_MIX = 0
N_GATE = N_MIX + 8 * PAIRS
N_BR = N_GATE + NB * DC
N_OUT = N_BR + NB * DC // 2
N_QRY = N_OUT + DC
N_U0 = N_QRY + HP
N_UV = N_U0 + EG
N_VL = N_UV + 2 * EG * (NG - 1)
N_PT = N_VL + EG
N_PLE = N_PT + 4
T = N_PLE + DC
assert T % RING == 0 and N_U0 % RING == 4

V_MIX = 0
V_BR = V_MIX + 8 * PAIRS
V_OUT = V_BR + NB * DC
V_QRY = V_OUT + DC
V_EXP = V_QRY + HP
V_PJ = V_EXP + NG * DC
V_ALL = V_PJ + DC
A_GATE, A_EXP, A_PLE = 0, NB * DC, NB * DC + NK
A_ALL = A_PLE + DC
assert V_EXP % 4 == 0 and V_ALL % 4 == 0

C_GAIN = 0
C_QG = C_GAIN + DEPTH * 3 * DC
C_KG = C_QG + DEPTH
C_CW = C_KG + DEPTH
C_PS = C_CW + DEPTH * GROUPS * 3
C_WIN = C_PS + DEPTH * GROUPS
C_CNT = C_WIN + GROUPS
C_EPS = C_CNT + GROUPS * 16
C_QEPS = C_EPS + 1
NVEC = C_QEPS + 1

TB = 32
NTB = SEQ // TB
QUADS = SEQ // 4


VO_ALL = (NG + 1) * (DC - 1)
POOL_LAYER = QUADS
DVE_LAYER, DVE_PAIR, DVE_TOPK = 152, 11, 22
LOWEST = -3.0e38


class Steps:

    def __init__(self, eng, sem, passed):
        self.eng, self.sem, self.base, self.k, self.passed = eng, sem, 0, 0, passed

    def link(self, ins, apart=False):
        self.k += 1
        ins.then_inc(self.sem, 1)
        self.eng.wait_ge(self.sem, self.base + self.k)
        if apart:
            self.eng.sem_inc(self.passed, 1)

    @contextmanager
    def loop(self, trips, per):
        base, k = self.base, self.k
        with self.eng.Fori(0, trips) as i:
            self.base, self.k = i * per + (base + k), 0
            yield i
            assert self.k == per, f"steps in this loop: {self.k}"
        self.base, self.k = base, k + trips * per


def trunk_kernel(nc, xT, stream, keys, vec, out):
    f32, f32r, u32 = mybir.dt.float32, mybir.dt.float32r, mybir.dt.uint32
    ALU, ACT, AX = mybir.AluOpType, mybir.ActivationFunctionType, mybir.AxisListType
    gate_table = nc.dram_tensor("gate_table", (NTB, P, NK * TB), f32, kind="Internal").ap()

    top = [16512]

    def area(size):
        top[0] += size
        return top[0] - size

    def sb(name, off, shape, dt=f32):
        return nc.alloc_sbuf_tensor_at(name, shape, dt, offset=off)

    KB = 1024
    o_h, o_c, o_raw, o_ring, o_x = area(16 * KB), area(4 * KB), area(16 * KB), area(64 * KB), area(32 * KB)
    o_r, o_t, o_b = area(32 * KB), area(19 * KB), area(24 * KB)
    assert top[0] <= 229368, top[0]

    hT = sb("hT", o_h, [P, DC, SEQ])
    ident = sb("ident", o_c, [P, P])
    ones = sb("ones", o_c + 512, [P, P])
    headones = sb("headones", o_c + 1024, [P, P])
    negtri = sb("negtri", o_c + 1536, [P, P])
    negones = sb("negones", o_c + 2048, [P, P])
    iota = sb("iota", o_c + 2560, [P, NK])
    vt = sb("vt", o_c + 3072, [P, NVEC])
    raw = [sb(f"raw{i}", o_raw + 4 * KB * i, [P, 1024]) for i in range(RAW)]
    hi = [sb(f"hi{i}", o_ring + 8 * KB * i, [P, 1024], f32r) for i in range(RING)]
    lo = [sb(f"lo{i}", o_ring + 8 * KB * i + 4 * KB, [P, 1024], f32r) for i in range(RING)]
    xh = sb("xh", o_x, [P, DC, SEQ], f32r)
    xl = sb("xl", o_x + 16 * KB, [P, DC, SEQ], f32r)
    brh = sb("brh", o_x, [P, 2, GROUPS, SEQ], f32r)
    brl = sb("brl", o_x + 16 * KB, [P, 2, GROUPS, SEQ], f32r)
    sq = sb("sq", o_t, [P, 2, SEQ])
    xt = sb("xt", o_t + 4 * KB, [P, 2, SEQ])
    rs = sb("rs", o_t + 8 * KB, [P, SEQ])
    attE = sb("attE", o_r, [P, NBLK, SEQ])
    attS = sb("attS", o_r + 8 * KB, [P, NBLK, SEQ])
    attW = sb("attW", o_r + 16 * KB, [P, NBLK, SEQ])
    qb = sb("qb", o_r + 24 * KB, [P, SEQ])
    kb = sb("kb", o_r + 26 * KB, [P, SEQ])
    vb = sb("vb", o_r + 28 * KB, [P, NBLK, P])
    vT = sb("vT", o_r + 30 * KB, [P, SEQ])
    qrs = sb("qrs", o_t, [P, SEQ])
    ksq = sb("ksq", o_t + 2 * KB, [P, SEQ])
    ccb = sb("ccb", o_t + 4 * KB, [P, SEQ])
    uc = sb("uc", o_t + 6 * KB, [P, 2 + SEQ])
    pw = sb("pw", o_t + 8256, [P, 5, 16 + SEQ])
    pfirst = sb("pfirst", o_t + 8256 + 10560, [P, 16])
    ph = sb("ph", o_r, [P, SEQ], f32r)
    pl = sb("pl", o_r + 2 * KB, [P, SEQ], f32r)
    BR = sb("BR", o_b, [P, NB, GROUPS, SEQ])
    G3 = sb("G3", o_r, [P, NB, DC, SEQ])
    mh = sb("mh", o_r + 16 * KB, [P, DC, SEQ], f32r)
    ml = sb("ml", o_r + 32 * KB, [P, DC, SEQ], f32r)
    keyh = sb("keyh", o_r, [P, HP, NK], f32r)
    keyl = sb("keyl", o_r + 8 * KB, [P, HP, NK], f32r)
    qh = sb("qh", o_r + 16 * KB, [P, 2, SEQ], f32r)
    ql = sb("ql", o_r + 20 * KB, [P, 2, SEQ], f32r)
    keyraw = sb("keyraw", o_r + 24 * KB, [P, HP, NK])
    SC = sb("SC", o_t, [P, NBLK, HP, NK])
    tabs = sb("tabs", o_t + 32 * KB, [P, 3, SEQ])
    S1 = sb("S1", o_r + 24 * KB, [P, HP, NK])
    S2 = sb("S2", o_r, [P, HP, NK])
    eqj = sb("eqj", o_r, [P, PH, TOPK, TOPK])
    cand = sb("cand", o_r + 8 * KB, [P, PH, TOPK, TOPK])
    eqi = sb("eqi", o_r + 8 * KB, [P, PH, TOPK, TOPK])
    cand2 = sb("cand2", o_r, [P, PH, TOPK * TOPK])
    o_s = o_r + 16 * KB
    hv = sb("hv", o_s, [P, HP, TOPK])
    hx = sb("hx", o_s + KB, [P, HP, TOPK], u32)
    hxf = sb("hxf", o_s + 2 * KB, [P, HP, TOPK])
    tv = sb("tv", o_s + 3 * KB, [P, PH, TOPK])
    tx = sb("tx", o_s + 3 * KB + 512, [P, PH, TOPK], u32)
    txa = sb("txa", o_s + 4 * KB, [P, 2, PH, TOPK], u32)
    txf = sb("txf", o_s + 5 * KB, [P, 2, PH, TOPK])
    ex = sb("ex", o_s + 6 * KB, [P, PH, TOPK])
    ssum = sb("ssum", o_t + 38 * KB, [P, 2, PH])
    slot3 = sb("slot3", o_s + 6 * KB + 512, [P, 3, PH, TOPK])
    LB = sb("LB", o_r + 24 * KB, [P, 2, 4, NK])
    RB = sb("RB", o_r + 28 * KB, [P, 2, 4, NK])
    cols = sb("cols", o_t + 38 * KB + 64, [P, 2, 4])
    stage = sb("stage", o_t, [P, 2, NK, TB])
    ah = sb("ah", o_r, [P, 2, EG, SEQ], f32r)
    al = sb("al", o_r + 16 * KB, [P, 2, EG, SEQ], f32r)
    gb = sb("gb", o_t, [P, 2, NTB, EG * TB])
    ge = sb("ge", o_t + 16 * KB, [P, 2, SEQ])
    af = sb("af", o_t + 20 * KB, [P, 2, SEQ])
    pj = sb("pj", o_t + 24 * KB, [P, DC, SEQ])

    ctx = ExitStack()
    with ctx:
        bank = [ctx.enter_context(nc.psum_tensor(f"bank{i}", [P, SEQ], f32)) for i in range(8)]

        def sem(name):
            return ctx.enter_context(nc.semaphore(name))

        x_in, vec_in, keys_in, out_done = sem("x_in"), sem("vec_in"), sem("keys_in"), sem("out_done")
        raw_in = [sem(f"raw_in{i}") for i in range(RAW)]
        hi_split = sem("hi_split")
        lo_split = sem("lo_split")
        tile_done = sem("tile_done")
        half_out = sem("half_out")
        v_out = sem("v_out")
        dve_evac = sem("dve_evac")
        act_evac = sem("act_evac")
        const_ready = sem("const_ready")
        passed = sem("passed")
        sq_ready, sq_used, root_ready = sem("sq_ready"), sem("sq_used"), sem("root_ready")
        xt_ready, xh_ready, xl_ready = sem("xt_ready"), sem("xh_ready"), sem("xl_ready")
        ple_added = sem("ple_added")
        qk_sq, qk_ssq, qk_root = sem("qk_sq"), sem("qk_ssq"), sem("qk_root")
        v_turned, v_ready = sem("v_turned"), sem("v_ready")
        z_ready, abs_ready, ln_ready, sp_ready = sem("z_ready"), sem("abs_ready"), sem("ln_ready"), sem("sp_ready")
        sp_masked, arg_ready, w_ready, w_masked = sem("sp_masked"), sem("arg_ready"), sem("w_ready"), sem("w_masked")
        pv_ready, pv_taken = sem("pv_ready"), sem("pv_taken")
        pooled, pooled_hi, pooled_lo = sem("pooled"), sem("pooled_hi"), sem("pooled_lo")
        br_hi, br_lo, mix_ready, mix_hi, mix_lo = sem("br_hi"), sem("br_lo"), sem("mix_ready"), sem("mix_hi"), sem("mix_lo")
        keys_hi, keys_lo, qh_ready, scores_out, sc_ready = sem("keys_hi"), sem("keys_lo"), sem("qh_ready"), sem("scores_out"), sem("sc_ready")
        top_ready, ex_ready, slots_ready, turned, tabs_ready = sem("top_ready"), sem("ex_ready"), sem("slots_ready"), sem("turned"), sem("tabs_ready")
        chunk_ready = sem("chunk_ready")
        row_hot, col_hot = sem("row_hot"), sem("col_hot")
        hot_used = sem("hot_used")
        staged = sem("staged")
        table_out = [sem("table_out0"), sem("table_out1")]
        gate_in = [sem("gate_in0"), sem("gate_in1")]
        a_ready, ah_ready, al_ready = sem("a_ready"), sem("ah_ready"), sem("al_ready")
        exp_ready, dve_step, pool_step = sem("exp_ready"), sem("dve_step"), sem("pool_step")

        block = ctx.enter_context(nc.Block())

        def apart(eng):
            eng.sem_inc(passed, 1)

        def number(l, k, i=0):
            return l * T + i * 8 + k, l * (T // RAW) + i * 2 + k // RAW

        def width(k):
            k = k % T
            return P if k < N_GATE and k % 8 == 7 else SEQ if k in (N_PT, N_PT + 1) else 1024

        @block.sync
        def _(sp):
            with sp.Fori(0, (DEPTH * T + AHEAD) // RAW) as i:
                for r in range(RAW):
                    sp.wait_ge(lo_split, i * RAW + r + 1)
                    sp.dma_start(raw[r][:, :], stream[bass.ds(i * RAW + r, 1), :, :].rearrange("a p n -> (a p) n"))\
                      .then_inc(raw_in[r], 16)
            sp.wait_ge(ple_added, 8 + DEPTH * DC)
            sp.dma_start(out, hT[:, :, :]).then_inc(out_done, 16)
            sp.wait_ge(out_done, 16)

        @block.gpsimd
        def _(pool):
            steps = Steps(pool, pool_step, passed)
            steps.link(pool.memset(ones[:, :], 1.0))
            steps.link(pool.memset(headones[:, :], 0.0))
            steps.link(pool.memset(negones[:, :], -1.0))
            steps.link(pool.iota(iota[:, :], [[1, NK]], base=0, channel_multiplier=0,
                                 allow_small_or_imprecise_dtypes=True))
            for r in (0, DH):
                steps.link(pool.memset(headones[r:r + DH, r:r + DH], 1.0))
            steps.link(pool.affine_select(out=ident[:, :], in_=ones[:, :], compare_op=ALU.is_equal, fill=0.0,
                                          base=0, pattern=[[-1, P]], channel_multiplier=1))
            pool.affine_select(out=negtri[:, :], in_=negones[:, :], compare_op=ALU.is_ge, fill=0.0,
                               base=0, pattern=[[-1, P]], channel_multiplier=1).then_inc(const_ready, 1)

            def keep_later(buf, sb_, done):
                d = buf[:, sb_, sb_ * P:(sb_ + 1) * P]
                pool.affine_select(out=d, in_=d, compare_op=ALU.is_gt, fill=0.0,
                                   base=0, pattern=[[1, P]], channel_multiplier=-1).then_inc(done, 1)

            with steps.loop(DEPTH, POOL_LAYER) as l:
                with pool.Fori(0, 2 * PAIRS) as h:
                    a = l * (8 * PAIRS) + h * 4
                    for i, s in enumerate(reversed(range(NBLK))):
                        pool.wait_ge(sp_ready, a + i + 1)
                        apart(pool)
                        keep_later(attS, s, sp_masked)
                    for i, s in enumerate(reversed(range(NBLK))):
                        pool.wait_ge(w_ready, a + i + 1)
                        apart(pool)
                        keep_later(attW, s, w_masked)
                pool.wait_ge(tabs_ready, (l + 1) * NBLK)
                apart(pool)
                with steps.loop(QUADS // 2, 2) as i:
                    for u in range(2):
                        pool.wait_ge(hot_used, l * QUADS + i * 2 + u + 1)
                        steps.link(pool.tensor_copy(cols[:, u, :], tabs[:, 1, bass.ds(i * 8 + u * 4, 4)]), True)
                        for q in range(4):
                            last = pool.tensor_scalar(RB[:, u, q, :], iota[:, :], cols[:, u, q:q + 1], None, ALU.is_equal)
                        last.then_inc(col_hot, 1)

        @block.scalar
        def _(act):
            act.dma_start(hT[:, :, :], xT).then_inc(x_in, 16)
            act.dma_start(vt[:, :], vec).then_inc(vec_in, 16)
            act.sem_inc(act_evac, 2)
            act.sem_inc(staged, 2)

            def split(l, k, i=0):
                n, turn = number(l, k, i)
                w = width(k)
                act.wait_ge(raw_in[k % RAW], turn * 16 + 16)
                act.wait_ge(tile_done, n + 1)
                act.activation(hi[k % RING][:, 0:w], raw[k % RAW][:, 0:w], ACT.Copy).then_inc(hi_split, 1)

            def norm(l, k):
                o = l * 3 + k
                for c in range(DC):
                    if k == 0:
                        act.wait_ge(ple_added, l * DC + c + 1)
                    elif k == 1:
                        act.wait_ge(dve_evac, 4 + l * V_ALL + V_OUT + c + 1)
                    else:
                        act.wait_ge(dve_evac, 4 + l * V_ALL + V_EXP + (NG - 1) * DC + c + 1)
                    act.wait_ge(sq_used, o * DC + c + 1)
                    act.activation(sq[:, c % 2, :], hT[:, c, :], ACT.Square).then_inc(sq_ready, 1)
                act.wait_ge(sq_used, 2 + o * DC + DC)
                act.activation(rs[:, :], bank[2][:, :], ACT.Sqrt, scale=1.0 / D, bias=vt[:, C_EPS:C_EPS + 1])\
                   .then_inc(root_ready, 1)
                for c in range(DC):
                    act.wait_ge(xt_ready, o * DC + c + 1)
                    act.activation(xh[:, c, :], xt[:, c % 2, :], ACT.Copy).then_inc(xh_ready, 1)

            act.wait_ge(x_in, 16)
            act.wait_ge(vec_in, 16)
            for k in range(AHEAD):
                split(0, k)
            with act.Fori(0, DEPTH) as l:
                norm(l, 0)
                with act.Fori(0, PAIRS) as b:
                    n0 = l * T + b * 8 + RING
                    s2 = l * (2 * PAIRS) + b * 2
                    act.wait_ge(tile_done, n0 + 1)
                    act.activation(ksq[:, :], bank[0][:, :], ACT.Square).then_inc(qk_sq, 1)
                    split(l, 4, b)
                    act.wait_ge(qk_ssq, s2 + 1)
                    act.activation(qrs[:, :], bank[2][:, :], ACT.Sqrt, bias=vt[:, C_QEPS:C_QEPS + 1])\
                       .then_inc(qk_root, 1)
                    act.wait_ge(tile_done, n0 + 2)
                    act.activation(ksq[:, :], bank[1][:, :], ACT.Square).then_inc(qk_sq, 1)
                    split(l, 5, b)
                    act.wait_ge(qk_ssq, s2 + 2)
                    act.activation(ksq[:, :], bank[3][:, :], ACT.Sqrt, scale=1.0 / DH, bias=vt[:, C_EPS:C_EPS + 1])\
                       .then_inc(qk_root, 1)
                    split(l, 6, b)
                    for h in range(2):
                        a = (s2 + h) * 4
                        for i, s in enumerate(reversed(range(NBLK))):
                            act.wait_ge(abs_ready, a + i + 1)
                            act.activation(attE[:, s, s * P:SEQ], attE[:, s, s * P:SEQ], ACT.Exp, scale=-1.0)\
                               .then_inc(exp_ready, 1)
                        for i, s in enumerate(reversed(range(NBLK))):
                            act.wait_ge(exp_ready, a + i + 1)
                            act.activation(attE[:, s, s * P:SEQ], attE[:, s, s * P:SEQ], ACT.Ln, bias=1.0)\
                               .then_inc(ln_ready, 1)
                        split(l, 7 if h == 0 else 9, b)
                        for i, s in enumerate(reversed(range(NBLK))):
                            act.wait_ge(arg_ready, a + i + 1)
                            act.activation(attW[:, s, s * P:SEQ], bank[4 + s][:, s * P:SEQ], ACT.Exp)\
                               .then_inc(w_ready, 1)
                        split(l, 8 if h == 0 else 10, b)
                    act.wait_ge(pooled, l * PAIRS + b + 1)
                    act.activation(ph[:, :], ccb[:, :], ACT.Copy).then_inc(pooled_hi, 1)
                    split(l, 11, b)
                act.wait_ge(dve_evac, 4 + l * V_ALL + V_BR)
                apart(act)
                with act.Fori(0, NB) as j:
                    for m in range(DC):
                        act.wait_ge(tile_done, RING + l * T + N_GATE + j * 8 + m + 1)
                        act.activation(G3[:, bass.ds(j, 1), m, :].rearrange("p a t -> p (a t)"), bank[4 + m % 2][:, :],
                                       ACT.Sigmoid).then_inc(act_evac, 1)
                        split(l, N_GATE + m + AHEAD, j)
                for j in range(NB):
                    if j < 2:
                        act.wait_ge(tile_done, RING + l * T + N_BR)
                    else:
                        act.wait_ge(tile_done, RING + l * T + N_BR + DC // 2)
                    act.activation(brh[:, j % 2, :, :], BR[:, j, :, :], ACT.Copy).then_inc(br_hi, 1)
                    if j > 0:
                        for k in range(DC // 2):
                            split(l, N_BR + (j - 1) * (DC // 2) + k + AHEAD)
                for m in range(DC):
                    if m % 2 == 0:
                        split(l, N_BR + DC + m // 2 + AHEAD)
                    act.wait_ge(mix_ready, l * DC + m + 1)
                    act.activation(mh[:, m, :], G3[:, 0, m, :], ACT.Copy).then_inc(mix_hi, 1)
                for m in range(DC):
                    split(l, N_OUT + m + AHEAD)
                act.wait_ge(tile_done, RING + l * T + N_QRY)
                act.dma_start(keyraw[:, :, :], keys[bass.ds(l, 1), :, :, :].rearrange("a p h k -> (a p) h k"))\
                   .then_inc(keys_in, 16)
                norm(l, 1)
                act.wait_ge(keys_in, l * 16 + 16)
                act.activation(keyh[:, :, :], keyraw[:, :, :], ACT.Copy).then_inc(keys_hi, 1)

                def take_scores(l, i, k):
                    act.wait_ge(scores_out, l * HP + i * 8 + k + 1)
                    act.activation(SC[:, :, bass.ds(i * 8 + k, 1), :].rearrange("p c a k -> p c (a k)"),
                                   bank[2 + k % 2][:, :].rearrange("p (c k) -> p c k", k=NK), ACT.Copy)\
                       .then_inc(sc_ready, 1)

                with act.Fori(0, HP // 8) as i:
                    for k in range(8):
                        act.wait_ge(tile_done, RING + l * T + N_QRY + i * 8 + k + 1)
                        act.activation(qh[:, k % 2, :], bank[k % 2][:, :], ACT.Copy).then_inc(qh_ready, 1)
                        split(l, N_QRY + k + AHEAD, i)
                        if k:
                            take_scores(l, i, k - 1)
                    take_scores(l, i, 7)
                act.wait_ge(keys_lo, l + 1)
                apart(act)
                with act.Fori(0, NBLK) as c:
                    act.wait_ge(sc_ready, (l + 1) * HP)
                    act.wait_ge(top_ready, l * NBLK + c + 1)
                    act.activation(S1[:, :, :], SC[:, bass.ds(c, 1), :, :].rearrange("p a h k -> p (a h) k"), ACT.Copy)\
                       .then_inc(chunk_ready, 1)
                    act.wait_ge(top_ready, l * NBLK + c + 2)
                    act.activation(ex[:, :, :], ex[:, :, :], ACT.Exp).then_inc(ex_ready, 1)
                act.wait_ge(tabs_ready, (l + 1) * NBLK)

                def stage_block(i, u):
                    for q in range(TB // 4):
                        n = i * (TB // 2) + (u * TB // 4 + q)
                        act.wait_ge(hot_used, 2 + l * QUADS + n + 1)
                        act.activation(stage[:, u, :, q * 4:q * 4 + 4],
                                       bank[6 + q % 2][:, :].rearrange("p (t k) -> p k t", k=NK), ACT.Copy)\
                           .then_inc(staged, 1)
                    act.wait_ge(staged, 2 + l * QUADS + i * (TB // 2) + (u + 1) * TB // 4)
                    act.dma_start(gate_table[bass.ds(i * 2 + u, 1), :, :].rearrange("a p n -> (a p) n"),
                                  stage[:, u, :, :].rearrange("p k t -> p (k t)")).then_inc(table_out[u], 16)

                for u in range(2):
                    stage_block(0, u)
                with act.Fori(1, NTB // 2) as i:
                    for u in range(2):
                        act.wait_ge(table_out[u], l * (NTB * 8) + i * 16)
                        stage_block(i, u)
                for u in range(2):
                    act.wait_ge(table_out[u], (l + 1) * (NTB * 8))

                def fetch(g, u):
                    act.dma_start(gb[:, u, :, :],
                                  gate_table[:, :, bass.ds(g * (EG * TB), EG * TB)].rearrange("b p n -> p b n"))\
                       .then_inc(gate_in[u], 16)

                def experts(g, u, k0, i=0):
                    for k in range(EG):
                        act.wait_ge(tile_done, RING + l * T + i * 8 + k0 + k + 1)
                        act.activation(ge[:, k % 2, :], bank[4 + k % 2][:, :], ACT.Gelu_apprx_tanh).then_inc(act_evac, 1)
                        split(l, k0 + k + AHEAD, i)
                        act.wait_ge(a_ready, l * NK + g * EG + k + 1)
                        act.activation(ah[:, u, k, :], af[:, k % 2, :], ACT.Copy).then_inc(ah_ready, 1)

                fetch(0, 0)
                fetch(1, 1)
                experts(0, 0, N_U0)
                with act.Fori(0, NG // 2 - 1) as i:
                    act.wait_ge(a_ready, l * NK + (i * 2 + 1) * EG)
                    fetch(i * 2 + 2, 0)
                    experts(i * 2 + 1, 1, N_UV, i * 2)
                    for k in range(EG):
                        split(l, N_UV + EG + k + AHEAD, i * 2)
                    act.wait_ge(a_ready, l * NK + (i * 2 + 2) * EG)
                    fetch(i * 2 + 3, 1)
                    experts(i * 2 + 2, 0, N_UV + 8, i * 2)
                    for k in range(EG):
                        split(l, N_UV + 8 + EG + k + AHEAD, i * 2)
                experts(NG - 1, 1, N_VL - 2 * EG)
                for k in range(EG):
                    split(l, N_VL - EG + k + AHEAD)
                for k in range(2 * EG):
                    split(l, N_VL + k + AHEAD)
                norm(l, 2)
                for m in range(DC):
                    act.wait_ge(tile_done, RING + l * T + N_PLE + m + 1)
                    if m >= 2:
                        act.wait_ge(ple_added, DC + l * DC + m - 1)
                    act.activation(ge[:, m % 2, :], bank[4 + m % 2][:, :], ACT.Sigmoid).then_inc(act_evac, 1)
                    split(l, N_PLE + m + AHEAD)

        @block.vector
        def _(dve):
            steps = Steps(dve, dve_step, passed)
            link = steps.link
            dve.sem_inc(lo_split, RAW)
            dve.sem_inc(dve_evac, 4)
            dve.sem_inc(ple_added, DC)
            dve.sem_inc(pv_taken, 1)
            dve.sem_inc(top_ready, 1)

            def split(l, k, i=0):
                n, _ = number(l, k, i)
                w = width(k)
                dve.wait_ge(hi_split, n + 1)
                dve.tensor_tensor(lo[k % RING][:, 0:w], raw[k % RAW][:, 0:w],
                                  hi[k % RING][:, 0:w].bitcast(f32), ALU.subtract).then_inc(lo_split, 1)

            def norm(l, k):
                o = l * 3 + k
                dve.wait_ge(root_ready, o + 1)
                link(dve.reciprocal(rs[:, :], rs[:, :]))

                def low(c):
                    dve.wait_ge(xh_ready, o * DC + c + 1)
                    dve.tensor_tensor(xl[:, c, :], xt[:, c % 2, :], xh[:, c, :].bitcast(f32), ALU.subtract)\
                       .then_inc(xl_ready, 1)

                for c in range(DC):
                    gain = vt[:, bass.ds(l * (3 * DC) + C_GAIN + k * DC + c, 1)]
                    if c >= 2:
                        dve.wait_ge(xl_ready, o * DC + c - 1)
                    dve.scalar_tensor_tensor(xt[:, c % 2, :], hT[:, c, :], gain, rs[:, :], ALU.mult, ALU.mult)\
                       .then_inc(xt_ready, 1)
                    if c:
                        low(c - 1)
                low(DC - 1)
                dve.wait_ge(xl_ready, o * DC + DC)
                apart(dve)

            dve.wait_ge(vec_in, 16)
            dve.wait_ge(x_in, 16)
            dve.wait_ge(const_ready, 1)
            for k in range(AHEAD):
                split(0, k)
            with steps.loop(DEPTH, DVE_LAYER) as l:
                norm(l, 0)
                dve.memset(uc[:, 0:2], 0.0)
                link(dve.memset(pw[:, :, 0:16], 0.0), True)
                with steps.loop(PAIRS, DVE_PAIR) as b:
                    n0 = l * T + b * 8 + RING
                    s1 = l * PAIRS + b
                    split(l, 4, b)
                    dve.wait_ge(qk_root, s1 * 2 + 1)
                    link(dve.reciprocal(qrs[:, :], qrs[:, :]))
                    dve.scalar_tensor_tensor(qb[:, :], bank[0][:, :], vt[:, bass.ds(l + C_QG, 1)], qrs[:, :],
                                             ALU.mult, ALU.mult).then_inc(dve_evac, 1)
                    split(l, 5, b)
                    dve.wait_ge(qk_root, s1 * 2 + 2)
                    link(dve.reciprocal(ksq[:, :], ksq[:, :]))
                    dve.scalar_tensor_tensor(kb[:, :], bank[1][:, :], vt[:, bass.ds(l + C_KG, 1)], ksq[:, :],
                                             ALU.mult, ALU.mult).then_inc(dve_evac, 1)
                    dve.wait_ge(tile_done, n0 + 3)
                    dve.tensor_copy(vT[:, :], bank[0][:, :]).then_inc(dve_evac, 1)
                    split(l, 6, b)

                    def softplus(h):
                        a = s1 * 8 + h * 4
                        for i, s in enumerate(reversed(range(NBLK))):
                            dve.wait_ge(z_ready, a + i + 1)
                            dve.tensor_scalar(attE[:, s, s * P:SEQ].bitcast(u32), bank[4 + s][:, s * P:SEQ].bitcast(u32),
                                              0x7FFFFFFF, None, ALU.bitwise_and).then_inc(abs_ready, 1)
                        if h == 0:
                            dve.wait_ge(v_turned, s1 + 1)
                            dve.tensor_copy(vb[:, :, :].rearrange("p s c -> p (s c)"), bank[2][:, :]).then_inc(v_ready, 1)
                        for i, s in enumerate(reversed(range(NBLK))):
                            dve.wait_ge(ln_ready, a + i + 1)
                            dve.scalar_tensor_tensor(attS[:, s, s * P:SEQ], bank[4 + s][:, s * P:SEQ], 0.0,
                                                     attE[:, s, s * P:SEQ], ALU.max, ALU.add).then_inc(sp_ready, 1)

                    softplus(0)
                    dve.wait_ge(tile_done, n0 + 4)
                    dve.tensor_copy(ccb[:, :], bank[1][:, :]).then_inc(dve_evac, 1)
                    split(l, 7, b)
                    dve.wait_ge(dve_evac, 4 + l * V_ALL + b * 8 + 4)
                    dve.wait_ge(tile_done, n0 + 5)
                    dve.tensor_tensor(uc[:, 2:2 + SEQ], bank[0][:, :], ccb[:, :], ALU.mult).then_inc(dve_evac, 1)
                    split(l, 8, b)
                    dve.wait_ge(dve_evac, 4 + l * V_ALL + b * 8 + 5)
                    y = BR[:, 1, bass.ds(b, 1), :].rearrange("p a t -> p (a t)")

                    def tap(j):
                        return vt[:, bass.ds(l * (GROUPS * 3) + b * 3 + (C_CW + j), 1)]

                    link(dve.tensor_scalar(y, uc[:, 0:SEQ], tap(0), None, ALU.mult))
                    for j in (1, 2):
                        link(dve.scalar_tensor_tensor(y, uc[:, j:j + SEQ], tap(j), y, ALU.mult, ALU.add))
                    softplus(1)
                    dve.wait_ge(tile_done, n0 + 6)
                    dve.tensor_tensor(y, bank[1][:, :], y, ALU.mult).then_inc(dve_evac, 1)
                    split(l, 9, b)
                    dve.wait_ge(tile_done, n0 + 7)
                    dve.tensor_copy(pw[:, 0, 16:], bank[0][:, :]).then_inc(dve_evac, 1)
                    dve.wait_ge(dve_evac, 4 + l * V_ALL + b * 8 + 7)
                    for w in range(GROUPS):
                        link(dve.tensor_tensor(pw[:, w + 1, 16:], pw[:, w, 16:], pw[:, w, 16 - (1 << w):16 + SEQ - (1 << w)],
                                               ALU.add))
                    total = pw[:, bass.ds(b + 1, 1), :].rearrange("p a t -> p (a t)")
                    link(dve.scalar_tensor_tensor(ccb[:, :], total[:, 16:], vt[:, bass.ds(b + C_WIN, 1)], pw[:, 0, 16:],
                                                  ALU.mult, ALU.subtract))
                    link(dve.tensor_tensor(pfirst[:, :], total[:, 16:32], vt[:, bass.ds(b * 16 + C_CNT, 16)], ALU.mult))
                    dve.tensor_tensor(ccb[:, 0:16], pfirst[:, :], pw[:, 0, 16:32], ALU.subtract).then_inc(pooled, 1)
                    split(l, 10, b)
                    dve.wait_ge(pooled_hi, s1 + 1)
                    dve.tensor_tensor(pl[:, :], ccb[:, :], ph[:, :].bitcast(f32), ALU.subtract).then_inc(pooled_lo, 1)
                    dve.wait_ge(pv_ready, s1 + 1)
                    dve.tensor_copy(BR[:, 0, bass.ds(b, 1), :].rearrange("p a t -> p (a t)"), bank[3][:, :])\
                       .then_inc(pv_taken, 1)
                    dve.wait_ge(tile_done, n0 + 8)
                    dve.tensor_scalar(BR[:, 2, bass.ds(b, 1), :].rearrange("p a t -> p (a t)"), bank[1][:, :],
                                      vt[:, bass.ds(l * GROUPS + b + C_PS, 1)], None, ALU.mult).then_inc(dve_evac, 1)
                    split(l, 11, b)
                with dve.Fori(0, NB) as j:
                    for m in range(DC):
                        split(l, N_GATE + m + AHEAD, j)
                dve.wait_ge(act_evac, 2 + l * A_ALL + NB * DC)

                def branch_low(j):
                    dve.wait_ge(br_hi, l * NB + j + 1)
                    dve.tensor_tensor(brl[:, j % 2, :, :], BR[:, j, :, :], brh[:, j % 2, :, :].bitcast(f32), ALU.subtract)\
                       .then_inc(br_lo, 1)

                branch_low(0)
                branch_low(1)
                for j in range(NB):
                    for m in range(DC):
                        k = j * (DC // 2) + m // 2
                        if m % 2:
                            dve.wait_ge(tile_done, RING + l * T + N_BR + k + 1)
                        else:
                            dve.wait_ge(half_out, l * (NB * DC // 2) + k + 1)
                        dve.tensor_tensor(G3[:, j, m, :], G3[:, j, m, :], bank[m % 2][:, :], ALU.mult).then_inc(dve_evac, 1)
                        if m % 2:
                            split(l, N_BR + k + AHEAD)
                        if j:
                            dve.wait_ge(dve_evac, 4 + l * V_ALL + V_BR + j * DC + m + 1)
                            add = dve.tensor_tensor(G3[:, 0, m, :], G3[:, 0, m, :], G3[:, j, m, :], ALU.add)
                            if j == 1:
                                link(add)
                            else:
                                add.then_inc(mix_ready, 1)
                                dve.wait_ge(mix_hi, l * DC + m + 1)
                                dve.tensor_tensor(ml[:, m, :], G3[:, 0, m, :], mh[:, m, :].bitcast(f32), ALU.subtract)\
                                   .then_inc(mix_lo, 1)
                    if j == 0:
                        branch_low(2)
                for m in range(DC):
                    dve.wait_ge(tile_done, RING + l * T + N_OUT + m + 1)
                    dve.tensor_tensor(hT[:, m, :], hT[:, m, :], bank[m % 2][:, :], ALU.add).then_inc(dve_evac, 1)
                    split(l, N_OUT + m + AHEAD)
                norm(l, 1)
                dve.wait_ge(keys_hi, l + 1)
                dve.tensor_tensor(keyl[:, :, :], keyraw[:, :, :], keyh[:, :, :].bitcast(f32), ALU.subtract).then_inc(keys_lo, 1)
                with dve.Fori(0, HP // 8) as i:
                    for k in range(8):
                        dve.wait_ge(qh_ready, l * HP + i * 8 + k + 1)
                        dve.tensor_tensor(ql[:, k % 2, :], bank[k % 2][:, :], qh[:, k % 2, :].bitcast(f32), ALU.subtract)\
                           .then_inc(dve_evac, 1)
                        split(l, N_QRY + k + AHEAD, i)
                with steps.loop(NBLK, DVE_TOPK) as c:
                    def batch(n, op):
                        for j in range(n):
                            last = op(j)
                        link(last, True)

                    dve.wait_ge(chunk_ready, l * NBLK + c + 1)
                    apart(dve)

                    def sc(j):
                        return S1[:, j, :]

                    batch(HP, lambda j: dve.max(hv[:, j, 0:8], sc(j)))
                    batch(HP, lambda j: dve.max_index(hx[:, j, 0:8], hv[:, j, 0:8], sc(j)))
                    batch(HP, lambda j: dve.match_replace(S2[:, j, :], hv[:, j, 0:8], sc(j), LOWEST))
                    batch(HP, lambda j: dve.max(hv[:, j, 8:16], S2[:, j, :]))
                    batch(HP, lambda j: dve.max_index(hx[:, j, 8:16], hv[:, j, 8:16], S2[:, j, :]))
                    link(dve.tensor_copy(hxf[:, :, :], hx[:, :, :]))
                    half = [hv[:, z::2, :] for z in range(2)]
                    full = [P, PH, TOPK, TOPK]
                    link(dve.tensor_tensor(cand[:, :, :, :], half[0].unsqueeze(3).to_broadcast(full),
                                           half[1].unsqueeze(2).to_broadcast(full), ALU.add), True)

                    def cd(j):
                        return cand[:, j, :, :].rearrange("p a b -> p (a b)")

                    batch(PH, lambda j: dve.max(tv[:, j, 0:8], cd(j)))
                    batch(PH, lambda j: dve.max_index(tx[:, j, 0:8], tv[:, j, 0:8], cd(j)))
                    batch(PH, lambda j: dve.match_replace(cand2[:, j, :], tv[:, j, 0:8], cd(j), LOWEST))
                    batch(PH, lambda j: dve.max(tv[:, j, 8:16], cand2[:, j, :]))
                    batch(PH, lambda j: dve.max_index(tx[:, j, 8:16], tv[:, j, 8:16], cand2[:, j, :]))
                    dve.tensor_tensor(ex[:, :, :], tv[:, :, :], tv[:, :, 0:1].to_broadcast([P, PH, TOPK]), ALU.subtract)\
                       .then_inc(top_ready, 1)
                    dve.tensor_scalar(txa[:, 0, :, :], tx[:, :, :], 4, None, ALU.logical_shift_right)
                    link(dve.tensor_scalar(txa[:, 1, :, :], tx[:, :, :], TOPK - 1, None, ALU.bitwise_and))
                    link(dve.tensor_copy(txf[:, :, :, :], txa[:, :, :, :]))
                    for z, eq in ((0, eqi), (1, eqj)):
                        link(dve.tensor_tensor(eq[:, :, :, :], txf[:, z, :, :].unsqueeze(3).to_broadcast(full),
                                               iota[:, 0:TOPK].unsqueeze(1).unsqueeze(1).to_broadcast(full), ALU.is_equal))
                        link(dve.tensor_tensor(eq[:, :, :, :], eq[:, :, :, :],
                                               hxf[:, z::2, :].unsqueeze(2).to_broadcast(full), ALU.mult))
                        link(dve.tensor_reduce(slot3[:, z, :, :], eq[:, :, :, :], AX.X, ALU.add))
                    dve.wait_ge(ex_ready, l * NBLK + c + 1)
                    link(dve.tensor_reduce(ssum[:, 0, :], ex[:, :, :], AX.X, ALU.add))
                    link(dve.reciprocal(ssum[:, 1, :], ssum[:, 0, :]))
                    dve.tensor_tensor(slot3[:, 2, :, :], ex[:, :, :], ssum[:, 1, :].unsqueeze(2).to_broadcast([P, PH, TOPK]),
                                      ALU.mult).then_inc(slots_ready, 1)
                    dve.wait_ge(turned, l * NBLK + c + 1)
                    dve.tensor_copy(tabs[:, :, bass.ds(c * P, P)],
                                    bank[4][:, 0:3 * P].rearrange("p (z t) -> p z t", z=3)).then_inc(tabs_ready, 1)
                dve.wait_ge(tabs_ready, (l + 1) * NBLK)
                apart(dve)
                with dve.Fori(0, QUADS // 2) as i:
                    for u in range(2):
                        dve.wait_ge(hot_used, l * QUADS + i * 2 + u + 1)
                        for q in range(4):
                            t = i * 8 + u * 4 + q
                            last = dve.tensor_scalar(LB[:, u, q, :], iota[:, :], tabs[:, 0, bass.ds(t, 1)],
                                                     tabs[:, 2, bass.ds(t, 1)], ALU.is_equal, ALU.mult)
                        last.then_inc(row_hot, 1)

                def experts(g, u, turn, k0, i=0):
                    dve.wait_ge(gate_in[u], l * (NG * 8) + turn * 16)
                    for k in range(EG):
                        dve.wait_ge(act_evac, 2 + l * A_ALL + A_EXP + g * EG + k + 1)
                        if k >= 2 or not (isinstance(g, int) and g == 0):
                            dve.wait_ge(al_ready, l * NK + g * EG + k - 1)
                        dve.tensor_tensor(af[:, k % 2, :].rearrange("p (b t) -> p b t", t=TB),
                                          ge[:, k % 2, :].rearrange("p (b t) -> p b t", t=TB),
                                          gb[:, u, :, k * TB:(k + 1) * TB], ALU.mult).then_inc(a_ready, 1)
                        split(l, k0 + k + AHEAD, i)
                        dve.wait_ge(ah_ready, l * NK + g * EG + k + 1)
                        dve.tensor_tensor(al[:, u, k, :], af[:, k % 2, :], ah[:, u, k, :].bitcast(f32), ALU.subtract)\
                           .then_inc(al_ready, 1)

                def gather(g, k0, i=0):
                    for d in range(DC):
                        if d < DC - 1:
                            dve.wait_ge(v_out, l * VO_ALL + g * (DC - 1) + d + 1)
                        else:
                            dve.wait_ge(tile_done, RING + l * T + i * 8 + k0 + EG)
                        dve.tensor_tensor(hT[:, d, :], hT[:, d, :], bank[d % 4][:, :], ALU.add).then_inc(dve_evac, 1)
                        if d % 2:
                            split(l, k0 + d // 2 + AHEAD, i)

                experts(0, 0, 1, N_U0)
                with dve.Fori(0, NG // 2 - 1) as i:
                    experts(i * 2 + 1, 1, i + 1, N_UV, i * 2)
                    gather(i * 2, N_UV + EG, i * 2)
                    experts(i * 2 + 2, 0, i + 2, N_UV + 8, i * 2)
                    gather(i * 2 + 1, N_UV + 8 + EG, i * 2)
                experts(NG - 1, 1, NG // 2, N_VL - 2 * EG)
                gather(NG - 2, N_VL - EG)
                gather(NG - 1, N_VL)
                for m in range(DC):
                    if m < DC - 1:
                        dve.wait_ge(v_out, l * VO_ALL + NG * (DC - 1) + m + 1)
                    else:
                        dve.wait_ge(tile_done, RING + l * T + N_PLE)
                    dve.tensor_copy(pj[:, m, :], bank[m % 2][:, :]).then_inc(dve_evac, 1)
                    if m < EG:
                        split(l, N_PT + m + AHEAD)
                norm(l, 2)
                for m in range(DC):
                    dve.wait_ge(act_evac, 2 + l * A_ALL + A_PLE + m + 1)
                    link(dve.tensor_tensor(pj[:, m, :], pj[:, m, :], ge[:, m % 2, :], ALU.mult))
                    dve.tensor_tensor(hT[:, m, :], hT[:, m, :], pj[:, m, :], ALU.add).then_inc(ple_added, 1)
                    split(l, N_PLE + m + AHEAD)

        @block.tensor
        def _(pe):
            pe.sem_inc(tile_done, RING)
            pe.sem_inc(sq_used, 2)
            pe.sem_inc(hot_used, 2)
            pe.wait_ge(const_ready, 1)

            def three(out_ap, w, mov_h, mov_l, first, last):
                slot, a = w
                for i, (st, mv) in enumerate(((hi, mov_h), (hi, mov_l), (lo, mov_h))):
                    ins = pe.matmul(out_ap, st[slot][:, a:a + P], mv, start=first and i == 0, stop=last and i == 2)
                return ins

            def dense(l, k, out_ap, mov, i=0):
                pe.wait_ge(lo_split, RAW + l * T + i * 8 + k + 1)
                for c in range(DC):
                    ins = three(out_ap, (k % RING, c * P), mov[0][:, c, :], mov[1][:, c, :], c == 0, c == DC - 1)
                ins.then_inc(tile_done, 1)

            def norm(l, k):
                o = l * 3 + k
                for c in range(DC):
                    pe.wait_ge(sq_ready, o * DC + c + 1)
                    pe.matmul(bank[2][:, :], ones[:, :], sq[:, c % 2, :], start=c == 0, stop=c == DC - 1)\
                      .then_inc(sq_used, 1)
                pe.wait_ge(xl_ready, o * DC + DC)
                apart(pe)

            with pe.Fori(0, DEPTH) as l:
                norm(l, 0)
                with pe.Fori(0, PAIRS) as b:
                    s1 = l * PAIRS + b
                    v0 = l * V_ALL + b * 8

                    def mix(k):
                        pe.wait_ge(dve_evac, v0 + k + 3)
                        dense(l, k, bank[k % 2][:, :], (xh, xl), b)

                    def ssq(z):
                        pe.wait_ge(qk_sq, s1 * 2 + z + 1)
                        pe.matmul(bank[2 + z][:, :], headones[:, :], ksq[:, :], start=True, stop=True).then_inc(qk_ssq, 1)

                    def scores(h):
                        r = h * DH
                        for s in reversed(range(NBLK)):
                            pe.matmul(bank[4 + s][:, s * P:SEQ], kb[r:r + DH, s * P:(s + 1) * P], qb[r:r + DH, s * P:SEQ],
                                      start=True, stop=True, skip_group_check=True).then_inc(z_ready, 1)

                    def remain(h):
                        a = s1 * 8 + h * 4
                        for i, s in enumerate(reversed(range(NBLK))):
                            pe.wait_ge(sp_masked, a + i + 1)
                            for j in range(s, NBLK):
                                ins = pe.matmul(bank[4 + s][:, j * P:SEQ], (negtri if j == s else negones)[:, :],
                                                attS[:, j, j * P:SEQ], start=False, stop=True, skip_group_check=True)
                            ins.then_inc(arg_ready, 1)

                    def weigh(h):
                        r = h * DH
                        pe.wait_ge(w_masked, s1 * 8 + h * 4 + 4)
                        for s in range(NBLK):
                            ins = pe.matmul(bank[3][r:r + DH, s * P:SEQ], vb[:, s, r:r + DH], attW[:, s, s * P:SEQ],
                                            start=s == 0, stop=s == NBLK - 1, skip_group_check=True)
                        return ins

                    mix(0)
                    mix(1)
                    ssq(0)
                    mix(2)
                    pe.wait_ge(pv_taken, s1 + 1)
                    ssq(1)
                    pe.wait_ge(dve_evac, v0 + 4 + 2)
                    scores(0)
                    pe.wait_ge(dve_evac, v0 + 4 + 3)
                    for s in range(NBLK):
                        ins = pe.transpose(bank[2][:, s * P:(s + 1) * P], vT[:, s * P:(s + 1) * P], ident[:, :])
                    ins.then_inc(v_turned, 1)
                    mix(3)
                    remain(0)
                    mix(4)
                    pe.wait_ge(v_ready, s1 + 1)
                    weigh(0)
                    scores(1)
                    mix(5)
                    remain(1)
                    mix(6)
                    weigh(1).then_inc(pv_ready, 1)
                    pe.wait_ge(pooled_lo, s1 + 1)
                    pe.wait_ge(dve_evac, v0 + 7 + 3)
                    pe.wait_ge(lo_split, RAW + l * T + b * 8 + 8)
                    three(bank[1][:, :], (7, 0), ph[:, :], pl[:, :], True, True).then_inc(tile_done, 1)
                with pe.Fori(0, NB) as j:
                    for m in range(DC):
                        pe.wait_ge(act_evac, l * A_ALL + j * DC + m + 1)
                        dense(l, N_GATE + m, bank[4 + m % 2][:, :], (xh, xl), j)
                for j in range(NB):
                    pe.wait_ge(br_lo, l * NB + j + 1)
                    for m in range(DC):
                        k = N_BR + j * (DC // 2) + m // 2
                        pe.wait_ge(dve_evac, 4 + l * V_ALL + V_BR + j * DC + m - 1)
                        if m % 2 == 0:
                            pe.wait_ge(lo_split, RAW + l * T + k + 1)
                        for c in range(GROUPS):
                            ins = three(bank[m % 2][:, :], (k % RING, (m % 2 * GROUPS + c) * P), brh[:, j % 2, c, :],
                                        brl[:, j % 2, c, :], c == 0, c == GROUPS - 1)
                        ins.then_inc(tile_done if m % 2 else half_out, 1)
                pe.wait_ge(mix_lo, l * DC + DC)
                for m in range(DC):
                    pe.wait_ge(dve_evac, 4 + l * V_ALL + V_OUT + m - 1)
                    dense(l, N_OUT + m, bank[m % 2][:, :], (mh, ml))
                norm(l, 1)
                pe.wait_ge(keys_lo, l + 1)
                apart(pe)

                def key_scores(i, k):
                    n = i * 8 + k
                    pe.wait_ge(dve_evac, 4 + l * V_ALL + V_QRY + n + 1)
                    if k >= 2:
                        pe.wait_ge(sc_ready, l * HP + n - 1)
                    for c in range(NBLK):
                        o = bank[2 + k % 2][:, c * P:(c + 1) * P]
                        kh, kl = (t[:, bass.ds(n, 1), :].rearrange("p a k -> p (a k)") for t in (keyh, keyl))
                        a, b_ = (t[:, k % 2, c * P:(c + 1) * P] for t in (qh, ql))
                        pe.matmul(o, a, kh, start=True, stop=False)
                        pe.matmul(o, a, kl, start=False, stop=False)
                        ins = pe.matmul(o, b_, kh, start=False, stop=True)
                    ins.then_inc(scores_out, 1)

                with pe.Fori(0, HP // 8) as i:
                    for k in range(8):
                        pe.wait_ge(dve_evac, 4 + l * V_ALL + V_QRY + i * 8 + k - 1)
                        dense(l, N_QRY + k, bank[k % 2][:, :], (xh, xl), i)
                        if k:
                            key_scores(i, k - 1)
                    key_scores(i, 7)
                with pe.Fori(0, NBLK) as c:
                    pe.wait_ge(slots_ready, l * NBLK + c + 1)
                    for z in range(3):
                        ins = pe.transpose(bank[4][:, z * P:(z + 1) * P], slot3[:, z, :, :].rearrange("p h k -> p (h k)"),
                                           ident[:, :])
                    ins.then_inc(turned, 1)
                with pe.Fori(0, QUADS // 2) as i:
                    for u in range(2):
                        n = l * QUADS + i * 2 + u
                        pe.wait_ge(row_hot, n + 1)
                        pe.wait_ge(col_hot, n + 1)
                        pe.wait_ge(staged, n + 1)
                        for q in range(4):
                            ins = pe.matmul(bank[6 + u][:, q * P:(q + 1) * P], RB[:, u, q, :], LB[:, u, q, :],
                                            start=True, stop=True)
                        ins.then_inc(hot_used, 1)

                def experts(g, k0, i=0):
                    for k in range(EG):
                        pe.wait_ge(act_evac, l * A_ALL + A_EXP + g * EG + k + 1)
                        dense(l, k0 + k, bank[4 + k % 2][:, :], (xh, xl), i)

                def values(g, u, k0, i=0):
                    pe.wait_ge(al_ready, l * NK + (g + 1) * EG)
                    pe.wait_ge(lo_split, RAW + l * T + i * 8 + k0 + EG)
                    for d in range(DC):
                        pe.wait_ge(dve_evac, l * V_ALL + V_EXP + g * DC + d + 1)
                        for k in range(EG):
                            ins = three(bank[d % 4][:, :], ((k0 + k) % RING, d * P), ah[:, u, k, :], al[:, u, k, :],
                                        k == 0, k == EG - 1)
                            if d == DC - 1:
                                ins.then_inc(tile_done, 1)
                        if d < DC - 1:
                            ins.then_inc(v_out, 1)

                experts(0, N_U0)
                with pe.Fori(0, NG // 2 - 1) as i:
                    experts(i * 2 + 1, N_UV, i * 2)
                    values(i * 2, 0, N_UV + EG, i * 2)
                    experts(i * 2 + 2, N_UV + 8, i * 2)
                    values(i * 2 + 1, 1, N_UV + 8 + EG, i * 2)
                experts(NG - 1, N_VL - 2 * EG)
                values(NG - 2, 0, N_VL - EG)
                values(NG - 1, 1, N_VL)
                pe.wait_ge(lo_split, RAW + l * T + N_PLE)
                for m in range(DC):
                    pe.wait_ge(dve_evac, 4 + l * V_ALL + V_PJ + m - 1)
                    for c in range(2):
                        pt, w = (N_PT + c) % RING, (N_PT + 2 + c) % RING
                        ins = three(bank[m % 2][:, :], (w, m * P), hi[pt][:, 0:SEQ], lo[pt][:, 0:SEQ], c == 0, c == 1)
                    if m < DC - 1:
                        ins.then_inc(v_out, 1)
                ins.then_inc(tile_done, 4)
                norm(l, 2)
                for m in range(DC):
                    pe.wait_ge(act_evac, l * A_ALL + A_PLE + m + 1)
                    dense(l, N_PLE + m, bank[4 + m % 2][:, :], (xh, xl))


def _tiles(w):
    k, n = w.shape
    return w.reshape(k // P, P, n // P, P).transpose(2, 1, 0, 3).reshape(n // P, P, -1)


def _stream(a, i):
    import numpy as np

    win = _tiles(a["w_in"][i])
    q, k, v, cb, cc, cu, pu = (win[4 * j:4 * j + 4] for j in range(7))
    pmap = np.zeros((GROUPS, P, 1024), win.dtype)
    pmap[:, :, 0:P] = a["pool_w"][i]
    mix = np.stack([q, k, v, cc, cu, cb, pu, pmap], axis=1).reshape(-1, P, 1024)
    br = a["w_branch"][i].reshape(NB, GROUPS, P, DC // 2, 2, P).transpose(0, 3, 2, 4, 1, 5).reshape(-1, P, 1024)
    u = _tiles(a["expert_u"][i].T).reshape(NG, EG, P, 1024)
    v_ = a["expert_v"][i].reshape(NG, EG, P, 1024)
    ex = [u[0]]
    for g in range(1, NG):
        ex += [u[g], v_[g - 1]]
    ex.append(v_[NG - 1])
    pt = np.zeros((2, P, 1024), win.dtype)
    pt[:, :, 0:SEQ] = a["p"][i, 0].T.reshape(2, P, SEQ)
    pj = a["w_ple_proj"][i].reshape(2, P, 1024)
    return [mix, win[28:], br, _tiles(a["w_out"][i]), _tiles(a["w_query"][i])] + ex + [pt, pj, _tiles(a["w_ple_gate"][i])]


def kernel(**inputs):
    import numpy as np
    import concourse.bacc as bacc
    from concourse.bass_utils import run_bass_kernel_spmd as run

    a = {k: np.asarray(v) for k, v in inputs.items()}
    xT = np.ascontiguousarray(a["x"][0].T.reshape(DC, P, SEQ).transpose(1, 0, 2))
    parts = [t for i in range(DEPTH) for t in _stream(a, i)] + [np.zeros((AHEAD, P, 1024), np.float32)]
    stream = np.concatenate(parts, axis=0)
    keys = np.ascontiguousarray(a["sub_keys"].reshape(DEPTH, HP, NK, P).transpose(0, 3, 1, 2))
    vec = np.zeros((P, NVEC), np.float32)
    gains = np.stack([a["norm_mix"], a["norm_ffn"], a["norm_ple"]], axis=1)
    vec[:, C_GAIN:C_QG] = gains.reshape(-1, P).T
    for z, name in ((C_QG, "q_norm"), (C_KG, "k_norm")):
        vec[:, z:z + DEPTH] = np.concatenate([a[name]] * 2, axis=1).T
    vec[:, C_CW:C_PS] = a["conv_w"].reshape(DEPTH, 3, GROUPS, P).transpose(3, 0, 2, 1).reshape(P, -1)
    vec[:, C_PS:C_WIN] = a["pool_scale"].reshape(-1, P).T
    for g in range(GROUPS):
        size = 2 << g
        vec[:, C_WIN + g] = 1.0 / size
        vec[:, C_CNT + 16 * g:C_CNT + 16 * g + 16] = [1.0 / min(t + 1, size) for t in range(16)]
    vec[:, C_EPS], vec[:, C_QEPS] = EPS, EPS * DH
    ins = {"xT": xT, "stream": stream, "keys": keys, "vec": vec}
    nc = bacc.Bacc("TRN2", target_bir_lowering=False, num_devices=1)
    aps = [nc.dram_tensor(f"in_{k}", v.shape, mybir.dt.from_np(v.dtype), kind="ExternalInput").ap() for k, v in ins.items()]
    out = nc.dram_tensor("out_0", (P, DC, SEQ), mybir.dt.float32, kind="ExternalOutput").ap()
    trunk_kernel(nc, *aps, out)
    r = run(nc, [{f"in_{k}": v for k, v in ins.items()}], core_ids=[0])
    got = r.results[0]["out_0"]
    return np.ascontiguousarray(got.transpose(1, 0, 2).reshape(D, SEQ).T).reshape(1, SEQ, D)
```

```python
import concourse.bass as bass
from concourse import mybir
from contextlib import ExitStack, contextmanager

P = 128
D, SEQ, DEPTH = 1024, 512, 2
DC = D // P
DH, SCALE_ROOT = 64, 8.0
NBLK = SEQ // P
PAIRS = 4
GROUPS = 4
NB = 3
HP, NK, TOPK = 16, 128, 16
PH = HP // 2
SLOTS = PH * TOPK
EPS = 1e-6

RING, RAW, AHEAD = 8, 4, 4
EG = 4
NG = NK // EG
N_MIX = 0
N_GATE = N_MIX + 8 * PAIRS
N_BR = N_GATE + NB * DC
N_OUT = N_BR + NB * DC // 2
N_QRY = N_OUT + DC
EARLY = 9
LAST_E = 2 * (EARLY - 1)
N_EY = N_QRY + HP
N_1 = N_EY + EARLY * EG
TURNS1 = LAST_E // 4
N_2 = N_1 + TURNS1 * 6 * EG
TURNS2 = (NG - LAST_E - 2) // 2
N_VL = N_2 + TURNS2 * 4 * EG + 2 * EG
N_PT = N_VL + EG
N_PLE = N_PT + 4
T = N_PLE + DC
assert T % RING == 0 and N_EY % RING == 4 and N_1 % RING == 0 and NG - LAST_E == 2 * TURNS2 + 2

V_MIX = 0
V_BR = V_MIX + 8 * PAIRS
V_OUT = V_BR + NB * DC
V_QRY = V_OUT + DC
V_EXP = V_QRY + HP
V_PJ = V_EXP + NG * DC
V_ALL = V_PJ + DC
A_EY = NB * DC
A_1 = A_EY + EARLY * EG
A_2 = A_1 + TURNS1 * 2 * EG
A_PLE = A_EY + NK
A_ALL = A_PLE + DC
assert V_EXP % 4 == 0 and V_ALL % 4 == 0

C_GAIN = 0
C_QG = C_GAIN + DEPTH * 3 * DC
C_KG = C_QG + DEPTH
C_CW = C_KG + DEPTH
C_PS = C_CW + DEPTH * GROUPS * 3
C_WIN = C_PS + DEPTH * GROUPS
C_CNT = C_WIN + GROUPS
C_EPS = C_CNT + GROUPS * 16
C_QEPS = C_EPS + 1
NVEC = C_QEPS + 1

TB = 32
NTB = SEQ // TB
QUADS = SEQ // 4


VO_ALL = (NG + 1) * (DC - 1)
DVE_LAYER, DVE_PAIR, DVE_TOPK = 152, 11, 22
LOWEST = -3.0e38


class Steps:

    def __init__(self, eng, sem, passed):
        self.eng, self.sem, self.base, self.k, self.passed = eng, sem, 0, 0, passed

    def link(self, ins, apart=False):
        self.k += 1
        ins.then_inc(self.sem, 1)
        self.eng.wait_ge(self.sem, self.base + self.k)
        if apart:
            self.eng.sem_inc(self.passed, 1)

    @contextmanager
    def loop(self, trips, per):
        base, k = self.base, self.k
        with self.eng.Fori(0, trips) as i:
            self.base, self.k = i * per + (base + k), 0
            yield i
            assert self.k == per, f"steps in this loop: {self.k}"
        self.base, self.k = base, k + trips * per


def trunk_kernel(nc, xT, stream, keys, vec, out):
    f32, f32r, u32 = mybir.dt.float32, mybir.dt.float32r, mybir.dt.uint32
    ALU, ACT, AX = mybir.AluOpType, mybir.ActivationFunctionType, mybir.AxisListType
    gate_table = nc.dram_tensor("gate_table", (NTB, P, NK * TB), f32, kind="Internal").ap()
    early = nc.dram_tensor("early", (P, EARLY * EG, SEQ), f32, kind="Internal").ap()

    top = [16512]

    def area(size):
        top[0] += size
        return top[0] - size

    def sb(name, off, shape, dt=f32):
        return nc.alloc_sbuf_tensor_at(name, shape, dt, offset=off)

    KB = 1024
    o_h, o_c, o_raw, o_ring, o_x = area(16 * KB), area(4 * KB), area(16 * KB), area(64 * KB), area(32 * KB)
    o_r, o_t, o_b = area(32 * KB), area(19 * KB), area(24 * KB)
    assert top[0] <= 229368, top[0]

    hT = sb("hT", o_h, [P, DC, SEQ])
    ident = sb("ident", o_c, [P, P])
    ones = sb("ones", o_c + 512, [P, P])
    headones = sb("headones", o_c + 1024, [P, P])
    negtri = sb("negtri", o_c + 1536, [P, P])
    negones = sb("negones", o_c + 2048, [P, P])
    iota = sb("iota", o_c + 2560, [P, NK])
    vt = sb("vt", o_c + 3072, [P, NVEC])
    raw = [sb(f"raw{i}", o_raw + 4 * KB * i, [P, 1024]) for i in range(RAW)]
    hi = [sb(f"hi{i}", o_ring + 8 * KB * i, [P, 1024], f32r) for i in range(RING)]
    lo = [sb(f"lo{i}", o_ring + 8 * KB * i + 4 * KB, [P, 1024], f32r) for i in range(RING)]
    xh = sb("xh", o_x, [P, DC, SEQ], f32r)
    xl = sb("xl", o_x + 16 * KB, [P, DC, SEQ], f32r)
    brh = sb("brh", o_x, [P, 2, GROUPS, SEQ], f32r)
    brl = sb("brl", o_x + 16 * KB, [P, 2, GROUPS, SEQ], f32r)
    sq = sb("sq", o_t, [P, 2, SEQ])
    xt = sb("xt", o_t + 4 * KB, [P, 2, SEQ])
    rs = sb("rs", o_t + 8 * KB, [P, SEQ])
    attE = sb("attE", o_r, [P, NBLK, SEQ])
    attS = sb("attS", o_r + 8 * KB, [P, NBLK, SEQ])
    attW = sb("attW", o_r + 16 * KB, [P, NBLK, SEQ])
    qb = sb("qb", o_r + 24 * KB, [P, SEQ])
    kb = sb("kb", o_r + 26 * KB, [P, SEQ])
    vb = sb("vb", o_r + 28 * KB, [P, NBLK, P])
    vT = sb("vT", o_r + 30 * KB, [P, SEQ])
    qrs = sb("qrs", o_t, [P, SEQ])
    ksq = sb("ksq", o_t + 2 * KB, [P, SEQ])
    ccb = sb("ccb", o_t + 4 * KB, [P, SEQ])
    uc = sb("uc", o_t + 6 * KB, [P, 2 + SEQ])
    pw = sb("pw", o_t + 8256, [P, 5, 16 + SEQ])
    pfirst = sb("pfirst", o_t + 8256 + 10560, [P, 16])
    ph = sb("ph", o_r, [P, SEQ], f32r)
    pl = sb("pl", o_r + 2 * KB, [P, SEQ], f32r)
    BR = sb("BR", o_b, [P, NB, GROUPS, SEQ])
    G3 = sb("G3", o_r, [P, NB, DC, SEQ])
    mh = sb("mh", o_r + 16 * KB, [P, DC, SEQ], f32r)
    ml = sb("ml", o_r + 32 * KB, [P, DC, SEQ], f32r)
    keyh = sb("keyh", o_r, [P, HP, NK], f32r)
    keyl = sb("keyl", o_r + 8 * KB, [P, HP, NK], f32r)
    qh = sb("qh", o_r + 16 * KB, [P, 2, SEQ], f32r)
    ql = sb("ql", o_r + 20 * KB, [P, 2, SEQ], f32r)
    keyraw = sb("keyraw", o_r + 24 * KB, [P, HP, NK])
    SC = sb("SC", o_t, [P, NBLK, HP, NK])
    tabs = sb("tabs", o_t + 32 * KB, [P, 3, SEQ])
    S1 = sb("S1", o_r + 24 * KB, [P, HP, NK])
    S2 = sb("S2", o_r, [P, HP, NK])
    eqj = sb("eqj", o_r, [P, PH, TOPK, TOPK])
    cand = sb("cand", o_r + 8 * KB, [P, PH, TOPK, TOPK])
    eqi = sb("eqi", o_r + 8 * KB, [P, PH, TOPK, TOPK])
    cand2 = sb("cand2", o_r, [P, PH, TOPK * TOPK])
    o_s = o_r + 16 * KB
    hv = sb("hv", o_s, [P, HP, TOPK])
    hx = sb("hx", o_s + KB, [P, HP, TOPK], u32)
    hxf = sb("hxf", o_s + 2 * KB, [P, HP, TOPK])
    tv = sb("tv", o_s + 3 * KB, [P, PH, TOPK])
    tx = sb("tx", o_s + 3 * KB + 512, [P, PH, TOPK], u32)
    txa = sb("txa", o_s + 4 * KB, [P, 2, PH, TOPK], u32)
    txf = sb("txf", o_s + 5 * KB, [P, 2, PH, TOPK])
    ex = sb("ex", o_s + 6 * KB, [P, PH, TOPK])
    ssum = sb("ssum", o_t + 38 * KB, [P, 2, PH])
    slot3 = sb("slot3", o_s + 6 * KB + 512, [P, 3, PH, TOPK])
    LB = sb("LB", o_r + 24 * KB, [P, 2, 4, NK])
    RB = sb("RB", o_r + 28 * KB, [P, 2, 4, NK])
    eo = sb("eo", o_t + 39 * KB, [P, 2, SEQ])
    stage = sb("stage", o_t, [P, 2, NK, TB])
    ah = sb("ah", o_r, [P, 2, EG, SEQ], f32r)
    al = sb("al", o_r + 16 * KB, [P, 2, EG, SEQ], f32r)
    gb = sb("gb", o_t, [P, 2, NTB, EG * TB])
    ge = sb("ge", o_t + 16 * KB, [P, 2, SEQ])
    af = sb("af", o_t + 20 * KB, [P, 2, SEQ])
    eb = sb("eb", o_t + 24 * KB, [P, EG, SEQ])
    pj = sb("pj", o_t + 24 * KB, [P, DC, SEQ])

    ctx = ExitStack()
    with ctx:
        bank = [ctx.enter_context(nc.psum_tensor(f"bank{i}", [P, SEQ], f32)) for i in range(8)]

        def sem(name):
            return ctx.enter_context(nc.semaphore(name))

        x_in, vec_in, keys_in, out_done = sem("x_in"), sem("vec_in"), sem("keys_in"), sem("out_done")
        raw_in = [sem(f"raw_in{i}") for i in range(RAW)]
        hi_split = sem("hi_split")
        lo_split = sem("lo_split")
        tile_done = sem("tile_done")
        half_out = sem("half_out")
        v_out = sem("v_out")
        dve_evac = sem("dve_evac")
        act_evac = sem("act_evac")
        const_ready = sem("const_ready")
        passed = sem("passed")
        sq_ready, sq_used, root_ready = sem("sq_ready"), sem("sq_used"), sem("root_ready")
        xt_ready, xh_ready, xl_ready = sem("xt_ready"), sem("xh_ready"), sem("xl_ready")
        ple_added = sem("ple_added")
        qk_sq, qk_ssq, qk_root = sem("qk_sq"), sem("qk_ssq"), sem("qk_root")
        v_turned, v_ready = sem("v_turned"), sem("v_ready")
        z_ready, abs_ready, ln_ready, sp_ready = sem("z_ready"), sem("abs_ready"), sem("ln_ready"), sem("sp_ready")
        sp_masked, arg_ready, w_ready, w_masked = sem("sp_masked"), sem("arg_ready"), sem("w_ready"), sem("w_masked")
        pv_ready, pv_taken = sem("pv_ready"), sem("pv_taken")
        pooled, pooled_hi, pooled_lo = sem("pooled"), sem("pooled_hi"), sem("pooled_lo")
        br_hi, br_lo, mix_ready, mix_hi, mix_lo = sem("br_hi"), sem("br_lo"), sem("mix_ready"), sem("mix_hi"), sem("mix_lo")
        keys_hi, keys_lo, qh_ready, scores_out, sc_ready = sem("keys_hi"), sem("keys_lo"), sem("qh_ready"), sem("scores_out"), sem("sc_ready")
        top_ready, ex_ready, slots_ready, turned, tabs_ready = sem("top_ready"), sem("ex_ready"), sem("slots_ready"), sem("turned"), sem("tabs_ready")
        chunk_ready = sem("chunk_ready")
        hot_ready = sem("hot_ready")
        hot_used = sem("hot_used")
        staged = sem("staged")
        table_out = [sem("table_out0"), sem("table_out1")]
        gate_in = [sem("gate_in0"), sem("gate_in1")]
        early_in, early_out = sem("early_in"), [sem("early_out0"), sem("early_out1")]
        a_ready, ah_ready, al_ready = sem("a_ready"), sem("ah_ready"), sem("al_ready")
        exp_ready, dve_step, pool_step = sem("exp_ready"), sem("dve_step"), sem("pool_step")

        block = ctx.enter_context(nc.Block())

        def apart(eng):
            eng.sem_inc(passed, 1)

        def number(l, k, i=0):
            return l * T + i * 8 + k, l * (T // RAW) + i * 2 + k // RAW

        def width(k):
            k = k % T
            return P if k < N_GATE and k % 8 == 7 else SEQ if k in (N_PT, N_PT + 1) else 1024

        @block.sync
        def _(sp):
            with sp.Fori(0, (DEPTH * T + AHEAD) // RAW) as i:
                for r in range(RAW):
                    sp.wait_ge(lo_split, i * RAW + r + 1)
                    sp.dma_start(raw[r][:, :], stream[bass.ds(i * RAW + r, 1), :, :].rearrange("a p n -> (a p) n"))\
                      .then_inc(raw_in[r], 16)
            sp.wait_ge(ple_added, 8 + DEPTH * DC)
            sp.dma_start(out, hT[:, :, :]).then_inc(out_done, 16)
            sp.wait_ge(out_done, 16)

        @block.gpsimd
        def _(pool):
            steps = Steps(pool, pool_step, passed)
            steps.link(pool.memset(ones[:, :], 1.0))
            steps.link(pool.memset(headones[:, :], 0.0))
            steps.link(pool.memset(negones[:, :], -1.0))
            steps.link(pool.iota(iota[:, :], [[1, NK]], base=0, channel_multiplier=0,
                                 allow_small_or_imprecise_dtypes=True))
            for r in (0, DH):
                steps.link(pool.memset(headones[r:r + DH, r:r + DH], 1.0))
            steps.link(pool.affine_select(out=ident[:, :], in_=ones[:, :], compare_op=ALU.is_equal, fill=0.0,
                                          base=0, pattern=[[-1, P]], channel_multiplier=1))
            pool.affine_select(out=negtri[:, :], in_=negones[:, :], compare_op=ALU.is_ge, fill=0.0,
                               base=0, pattern=[[-1, P]], channel_multiplier=1).then_inc(const_ready, 1)

            def keep_later(buf, sb_, done):
                d = buf[:, sb_, sb_ * P:(sb_ + 1) * P]
                pool.affine_select(out=d, in_=d, compare_op=ALU.is_gt, fill=0.0,
                                   base=0, pattern=[[1, P]], channel_multiplier=-1).then_inc(done, 1)

            with pool.Fori(0, DEPTH) as l:
                with pool.Fori(0, 2 * PAIRS) as h:
                    a = l * (8 * PAIRS) + h * 4
                    for i, s in enumerate(reversed(range(NBLK))):
                        pool.wait_ge(sp_ready, a + i + 1)
                        apart(pool)
                        keep_later(attS, s, sp_masked)
                    for i, s in enumerate(reversed(range(NBLK))):
                        pool.wait_ge(w_ready, a + i + 1)
                        apart(pool)
                        keep_later(attW, s, w_masked)
                def split(k, i=0):
                    n = l * T + i * 8 + k
                    pool.wait_ge(hi_split, n + 1)
                    pool.tensor_tensor(lo[k % RING][:, :], raw[k % RAW][:, :], hi[k % RING][:, :].bitcast(f32),
                                       ALU.subtract).then_inc(lo_split, 1)

                pool.wait_ge(lo_split, RAW + l * T + N_EY + AHEAD)
                for k in range(AHEAD):
                    split(N_EY + AHEAD + k)
                with pool.Fori(0, NBLK) as c:
                    for k in range(8):
                        split(N_EY + 2 * AHEAD + k, c)

        @block.scalar
        def _(act):
            act.dma_start(hT[:, :, :], xT).then_inc(x_in, 16)
            act.dma_start(vt[:, :], vec).then_inc(vec_in, 16)
            act.sem_inc(act_evac, 2)
            act.sem_inc(staged, 2)

            def split(l, k, i=0):
                n, turn = number(l, k, i)
                w = width(k)
                act.wait_ge(raw_in[k % RAW], turn * 16 + 16)
                act.wait_ge(tile_done, n + 1)
                act.activation(hi[k % RING][:, 0:w], raw[k % RAW][:, 0:w], ACT.Copy).then_inc(hi_split, 1)

            def norm(l, k):
                o = l * 3 + k
                for c in range(DC):
                    if k == 0:
                        act.wait_ge(ple_added, l * DC + c + 1)
                    elif k == 1:
                        act.wait_ge(dve_evac, 4 + l * V_ALL + V_OUT + c + 1)
                    else:
                        act.wait_ge(dve_evac, 4 + l * V_ALL + V_EXP + (NG - 1) * DC + c + 1)
                    act.wait_ge(sq_used, o * DC + c + 1)
                    act.activation(sq[:, c % 2, :], hT[:, c, :], ACT.Square).then_inc(sq_ready, 1)
                act.wait_ge(sq_used, 2 + o * DC + DC)
                act.activation(rs[:, :], bank[2][:, :], ACT.Sqrt, scale=1.0 / D, bias=vt[:, C_EPS:C_EPS + 1])\
                   .then_inc(root_ready, 1)
                for c in range(DC):
                    act.wait_ge(xt_ready, o * DC + c + 1)
                    act.activation(xh[:, c, :], xt[:, c % 2, :], ACT.Copy).then_inc(xh_ready, 1)

            act.wait_ge(x_in, 16)
            act.wait_ge(vec_in, 16)
            for k in range(AHEAD):
                split(0, k)
            with act.Fori(0, DEPTH) as l:
                norm(l, 0)
                with act.Fori(0, PAIRS) as b:
                    n0 = l * T + b * 8 + RING
                    s2 = l * (2 * PAIRS) + b * 2
                    act.wait_ge(tile_done, n0 + 1)
                    act.activation(ksq[:, :], bank[0][:, :], ACT.Square).then_inc(qk_sq, 1)
                    split(l, 4, b)
                    act.wait_ge(qk_ssq, s2 + 1)
                    act.activation(qrs[:, :], bank[2][:, :], ACT.Sqrt, bias=vt[:, C_QEPS:C_QEPS + 1])\
                       .then_inc(qk_root, 1)
                    act.wait_ge(tile_done, n0 + 2)
                    act.activation(ksq[:, :], bank[1][:, :], ACT.Square).then_inc(qk_sq, 1)
                    split(l, 5, b)
                    act.wait_ge(qk_ssq, s2 + 2)
                    act.activation(ksq[:, :], bank[3][:, :], ACT.Sqrt, scale=1.0 / DH, bias=vt[:, C_EPS:C_EPS + 1])\
                       .then_inc(qk_root, 1)
                    split(l, 6, b)
                    for h in range(2):
                        a = (s2 + h) * 4
                        for i, s in enumerate(reversed(range(NBLK))):
                            act.wait_ge(abs_ready, a + i + 1)
                            act.activation(attE[:, s, s * P:SEQ], attE[:, s, s * P:SEQ], ACT.Exp, scale=-1.0)\
                               .then_inc(exp_ready, 1)
                        for i, s in enumerate(reversed(range(NBLK))):
                            act.wait_ge(exp_ready, a + i + 1)
                            act.activation(attE[:, s, s * P:SEQ], attE[:, s, s * P:SEQ], ACT.Ln, bias=1.0)\
                               .then_inc(ln_ready, 1)
                        split(l, 7 if h == 0 else 9, b)
                        for i, s in enumerate(reversed(range(NBLK))):
                            act.wait_ge(arg_ready, a + i + 1)
                            act.activation(attW[:, s, s * P:SEQ], bank[4 + s][:, s * P:SEQ], ACT.Exp)\
                               .then_inc(w_ready, 1)
                        split(l, 8 if h == 0 else 10, b)
                    act.wait_ge(pooled, l * PAIRS + b + 1)
                    act.activation(ph[:, :], ccb[:, :], ACT.Copy).then_inc(pooled_hi, 1)
                    split(l, 11, b)
                act.wait_ge(dve_evac, 4 + l * V_ALL + V_BR)
                apart(act)
                with act.Fori(0, NB) as j:
                    for m in range(DC):
                        act.wait_ge(tile_done, RING + l * T + N_GATE + j * 8 + m + 1)
                        act.activation(G3[:, bass.ds(j, 1), m, :].rearrange("p a t -> p (a t)"), bank[4 + m % 2][:, :],
                                       ACT.Sigmoid).then_inc(act_evac, 1)
                        split(l, N_GATE + m + AHEAD, j)
                for j in range(NB):
                    if j < 2:
                        act.wait_ge(tile_done, RING + l * T + N_BR)
                    else:
                        act.wait_ge(tile_done, RING + l * T + N_BR + DC // 2)
                    act.activation(brh[:, j % 2, :, :], BR[:, j, :, :], ACT.Copy).then_inc(br_hi, 1)
                    if j > 0:
                        for k in range(DC // 2):
                            split(l, N_BR + (j - 1) * (DC // 2) + k + AHEAD)
                for m in range(DC):
                    if m % 2 == 0:
                        split(l, N_BR + DC + m // 2 + AHEAD)
                    act.wait_ge(mix_ready, l * DC + m + 1)
                    act.activation(mh[:, m, :], G3[:, 0, m, :], ACT.Copy).then_inc(mix_hi, 1)
                for m in range(DC):
                    split(l, N_OUT + m + AHEAD)
                act.wait_ge(tile_done, RING + l * T + N_QRY)
                act.dma_start(keyraw[:, :, :], keys[bass.ds(l, 1), :, :, :].rearrange("a p h k -> (a p) h k"))\
                   .then_inc(keys_in, 16)
                norm(l, 1)
                act.wait_ge(keys_in, l * 16 + 16)
                act.activation(keyh[:, :, :], keyraw[:, :, :], ACT.Copy).then_inc(keys_hi, 1)

                def take_scores(l, i, k):
                    act.wait_ge(scores_out, l * HP + i * 8 + k + 1)
                    act.activation(SC[:, :, bass.ds(i * 8 + k, 1), :].rearrange("p c a k -> p c (a k)"),
                                   bank[2 + k % 2][:, :].rearrange("p (c k) -> p c k", k=NK), ACT.Copy)\
                       .then_inc(sc_ready, 1)

                with act.Fori(0, HP // 8) as i:
                    for k in range(8):
                        act.wait_ge(tile_done, RING + l * T + N_QRY + i * 8 + k + 1)
                        act.activation(qh[:, k % 2, :], bank[k % 2][:, :], ACT.Copy).then_inc(qh_ready, 1)
                        split(l, N_QRY + k + AHEAD, i)
                        if k:
                            take_scores(l, i, k - 1)
                    take_scores(l, i, 7)
                act.wait_ge(keys_lo, l + 1)
                apart(act)

                def early_gelu(e, k, i=0):
                    act.wait_ge(tile_done, RING + l * T + i * 8 + k + 1)
                    act.activation(eo[:, k % 2, :], bank[4 + k % 2][:, :], ACT.Gelu_apprx_tanh).then_inc(act_evac, 1)
                    split(l, k + AHEAD, i)
                    act.wait_ge(act_evac, 2 + l * A_ALL + A_EY + e + 1)
                    act.dma_start(early[:, bass.ds(e, 1), :].rearrange("p a t -> p (a t)"), eo[:, k % 2, :])\
                       .then_inc(early_out[k % 2], 16)

                def early_flushed(l, e):
                    for u in range(2):
                        act.wait_ge(early_out[u], (l * (EARLY * EG) + e) * 8)

                act.wait_ge(sc_ready, (l + 1) * HP)
                for k in range(EG):
                    if k == 2:
                        early_flushed(l, 2)
                    early_gelu(0 + k, N_EY + k)
                early_flushed(l, EG)
                apart(act)
                with act.Fori(0, NBLK) as c:
                    act.wait_ge(top_ready, l * NBLK + c + 1)
                    act.activation(S1[:, :, :], SC[:, bass.ds(c, 1), :, :].rearrange("p a h k -> p (a h) k"), ACT.Copy)\
                       .then_inc(chunk_ready, 1)
                    for k in range(8):
                        if k >= 2:
                            act.wait_ge(early_out[k % 2], (l * (EARLY * EG) + c * 8 + EG + (k - k % 2)) * 8)
                        early_gelu(c * 8 + (EG + k), N_EY + EG + k, c)
                        if k == 6:
                            act.wait_ge(top_ready, l * NBLK + c + 2)
                            act.activation(ex[:, :, :], ex[:, :, :], ACT.Exp).then_inc(ex_ready, 1)
                    early_flushed(l, c * 8 + (EG + 8))
                    apart(act)
                act.wait_ge(tabs_ready, (l + 1) * NBLK)

                def stage_block(i, u):
                    for q in range(TB // 4):
                        n = i * (TB // 2) + (u * TB // 4 + q)
                        act.wait_ge(hot_used, 2 + l * QUADS + n + 1)
                        act.activation(stage[:, u, :, q * 4:q * 4 + 4],
                                       bank[6 + q % 2][:, :].rearrange("p (t k) -> p k t", k=NK), ACT.Copy)\
                           .then_inc(staged, 1)
                    act.wait_ge(staged, 2 + l * QUADS + i * (TB // 2) + (u + 1) * TB // 4)
                    act.dma_start(gate_table[bass.ds(i * 2 + u, 1), :, :].rearrange("a p n -> (a p) n"),
                                  stage[:, u, :, :].rearrange("p k t -> p (k t)")).then_inc(table_out[u], 16)

                for u in range(2):
                    stage_block(0, u)
                with act.Fori(1, NTB // 2) as i:
                    for u in range(2):
                        act.wait_ge(table_out[u], l * (NTB * 8) + i * 16)
                        stage_block(i, u)
                for u in range(2):
                    act.wait_ge(table_out[u], (l + 1) * (NTB * 8))

                def fetch(g, u):
                    act.dma_start(gb[:, u, :, :],
                                  gate_table[:, :, bass.ds(g * (EG * TB), EG * TB)].rearrange("b p n -> p b n"))\
                       .then_inc(gate_in[u], 16)

                def fetch_early(e):
                    act.dma_start(eb[:, :, :], early[:, bass.ds(e * EG, EG), :]).then_inc(early_in, 16)

                def high(g, u, k):
                    act.wait_ge(a_ready, l * NK + g * EG + k + 1)
                    act.activation(ah[:, u, k, :], af[:, k % 2, :], ACT.Copy).then_inc(ah_ready, 1)

                def experts(g, u, k0, i=0):
                    for k in range(EG):
                        act.wait_ge(tile_done, RING + l * T + i * 8 + k0 + k + 1)
                        act.activation(ge[:, k % 2, :], bank[4 + k % 2][:, :], ACT.Gelu_apprx_tanh).then_inc(act_evac, 1)
                        split(l, k0 + k + AHEAD, i)
                        high(g, u, k)

                def value_splits(k0, i=0):
                    for k in range(EG):
                        split(l, k0 + k + AHEAD, i)

                def used(g):
                    act.wait_ge(a_ready, l * NK + (g + 1) * EG)

                fetch_early(0)
                fetch(0, 0)
                fetch(1, 1)
                for k in range(EG):
                    high(0, 0, k)
                with act.Fori(0, TURNS1) as i:
                    used(i * 4)
                    fetch_early(i * 2 + 1)
                    fetch(i * 4 + 2, 0)
                    experts(i * 4 + 1, 1, N_1, i * 3)
                    used(i * 4 + 1)
                    fetch(i * 4 + 3, 1)
                    value_splits(N_1 + EG, i * 3)
                    act.wait_ge(tile_done, RING + l * T + i * 24 + N_1 + 2 * EG)
                    for k in range(EG):
                        high(i * 4 + 2, 0, k)
                    fetch_early(i * 2 + 2)
                    fetch(i * 4 + 4, 0)
                    value_splits(N_1 + 2 * EG, i * 3)
                    experts(i * 4 + 3, 1, N_1 + 3 * EG, i * 3)
                    used(i * 4 + 3)
                    fetch(i * 4 + 5, 1)
                    value_splits(N_1 + 4 * EG, i * 3)
                    act.wait_ge(tile_done, RING + l * T + i * 24 + N_1 + 5 * EG)
                    for k in range(EG):
                        high(i * 4 + 4, 0, k)
                    value_splits(N_1 + 5 * EG, i * 3)
                with act.Fori(0, TURNS2) as i:
                    used(i * 2 + LAST_E)
                    fetch(i * 2 + (LAST_E + 2), 0)
                    experts(i * 2 + (LAST_E + 1), 1, N_2, i * 2)
                    value_splits(N_2 + EG, i * 2)
                    used(i * 2 + (LAST_E + 1))
                    fetch(i * 2 + (LAST_E + 3), 1)
                    experts(i * 2 + (LAST_E + 2), 0, N_2 + 2 * EG, i * 2)
                    value_splits(N_2 + 3 * EG, i * 2)
                experts(NG - 1, 1, N_VL - 2 * EG)
                for k in range(EG):
                    split(l, N_VL - EG + k + AHEAD)
                for k in range(2 * EG):
                    split(l, N_VL + k + AHEAD)
                norm(l, 2)
                for m in range(DC):
                    act.wait_ge(tile_done, RING + l * T + N_PLE + m + 1)
                    if m >= 2:
                        act.wait_ge(ple_added, DC + l * DC + m - 1)
                    act.activation(ge[:, m % 2, :], bank[4 + m % 2][:, :], ACT.Sigmoid).then_inc(act_evac, 1)
                    split(l, N_PLE + m + AHEAD)

        @block.vector
        def _(dve):
            steps = Steps(dve, dve_step, passed)
            link = steps.link
            dve.sem_inc(lo_split, RAW)
            dve.sem_inc(dve_evac, 4)
            dve.sem_inc(ple_added, DC)
            dve.sem_inc(pv_taken, 1)
            dve.sem_inc(top_ready, 1)

            def split(l, k, i=0):
                n, _ = number(l, k, i)
                w = width(k)
                dve.wait_ge(hi_split, n + 1)
                dve.tensor_tensor(lo[k % RING][:, 0:w], raw[k % RAW][:, 0:w],
                                  hi[k % RING][:, 0:w].bitcast(f32), ALU.subtract).then_inc(lo_split, 1)

            def norm(l, k):
                o = l * 3 + k
                dve.wait_ge(root_ready, o + 1)
                link(dve.reciprocal(rs[:, :], rs[:, :]))

                def low(c):
                    dve.wait_ge(xh_ready, o * DC + c + 1)
                    dve.tensor_tensor(xl[:, c, :], xt[:, c % 2, :], xh[:, c, :].bitcast(f32), ALU.subtract)\
                       .then_inc(xl_ready, 1)

                for c in range(DC):
                    gain = vt[:, bass.ds(l * (3 * DC) + C_GAIN + k * DC + c, 1)]
                    if c >= 2:
                        dve.wait_ge(xl_ready, o * DC + c - 1)
                    dve.scalar_tensor_tensor(xt[:, c % 2, :], hT[:, c, :], gain, rs[:, :], ALU.mult, ALU.mult)\
                       .then_inc(xt_ready, 1)
                    if c:
                        low(c - 1)
                low(DC - 1)
                dve.wait_ge(xl_ready, o * DC + DC)
                apart(dve)

            dve.wait_ge(vec_in, 16)
            dve.wait_ge(x_in, 16)
            dve.wait_ge(const_ready, 1)
            for k in range(AHEAD):
                split(0, k)
            with steps.loop(DEPTH, DVE_LAYER) as l:
                norm(l, 0)
                dve.memset(uc[:, 0:2], 0.0)
                link(dve.memset(pw[:, :, 0:16], 0.0), True)
                with steps.loop(PAIRS, DVE_PAIR) as b:
                    n0 = l * T + b * 8 + RING
                    s1 = l * PAIRS + b
                    split(l, 4, b)
                    dve.wait_ge(qk_root, s1 * 2 + 1)
                    link(dve.reciprocal(qrs[:, :], qrs[:, :]))
                    dve.scalar_tensor_tensor(qb[:, :], bank[0][:, :], vt[:, bass.ds(l + C_QG, 1)], qrs[:, :],
                                             ALU.mult, ALU.mult).then_inc(dve_evac, 1)
                    split(l, 5, b)
                    dve.wait_ge(qk_root, s1 * 2 + 2)
                    link(dve.reciprocal(ksq[:, :], ksq[:, :]))
                    dve.scalar_tensor_tensor(kb[:, :], bank[1][:, :], vt[:, bass.ds(l + C_KG, 1)], ksq[:, :],
                                             ALU.mult, ALU.mult).then_inc(dve_evac, 1)
                    dve.wait_ge(tile_done, n0 + 3)
                    dve.tensor_copy(vT[:, :], bank[0][:, :]).then_inc(dve_evac, 1)
                    split(l, 6, b)

                    def softplus(h):
                        a = s1 * 8 + h * 4
                        for i, s in enumerate(reversed(range(NBLK))):
                            dve.wait_ge(z_ready, a + i + 1)
                            dve.tensor_scalar(attE[:, s, s * P:SEQ].bitcast(u32), bank[4 + s][:, s * P:SEQ].bitcast(u32),
                                              0x7FFFFFFF, None, ALU.bitwise_and).then_inc(abs_ready, 1)
                        if h == 0:
                            dve.wait_ge(v_turned, s1 + 1)
                            dve.tensor_copy(vb[:, :, :].rearrange("p s c -> p (s c)"), bank[2][:, :]).then_inc(v_ready, 1)
                        for i, s in enumerate(reversed(range(NBLK))):
                            dve.wait_ge(ln_ready, a + i + 1)
                            dve.scalar_tensor_tensor(attS[:, s, s * P:SEQ], bank[4 + s][:, s * P:SEQ], 0.0,
                                                     attE[:, s, s * P:SEQ], ALU.max, ALU.add).then_inc(sp_ready, 1)

                    softplus(0)
                    dve.wait_ge(tile_done, n0 + 4)
                    dve.tensor_copy(ccb[:, :], bank[1][:, :]).then_inc(dve_evac, 1)
                    split(l, 7, b)
                    dve.wait_ge(dve_evac, 4 + l * V_ALL + b * 8 + 4)
                    dve.wait_ge(tile_done, n0 + 5)
                    dve.tensor_tensor(uc[:, 2:2 + SEQ], bank[0][:, :], ccb[:, :], ALU.mult).then_inc(dve_evac, 1)
                    split(l, 8, b)
                    dve.wait_ge(dve_evac, 4 + l * V_ALL + b * 8 + 5)
                    y = BR[:, 1, bass.ds(b, 1), :].rearrange("p a t -> p (a t)")

                    def tap(j):
                        return vt[:, bass.ds(l * (GROUPS * 3) + b * 3 + (C_CW + j), 1)]

                    link(dve.tensor_scalar(y, uc[:, 0:SEQ], tap(0), None, ALU.mult))
                    for j in (1, 2):
                        link(dve.scalar_tensor_tensor(y, uc[:, j:j + SEQ], tap(j), y, ALU.mult, ALU.add))
                    softplus(1)
                    dve.wait_ge(tile_done, n0 + 6)
                    dve.tensor_tensor(y, bank[1][:, :], y, ALU.mult).then_inc(dve_evac, 1)
                    split(l, 9, b)
                    dve.wait_ge(tile_done, n0 + 7)
                    dve.tensor_copy(pw[:, 0, 16:], bank[0][:, :]).then_inc(dve_evac, 1)
                    dve.wait_ge(dve_evac, 4 + l * V_ALL + b * 8 + 7)
                    for w in range(GROUPS):
                        link(dve.tensor_tensor(pw[:, w + 1, 16:], pw[:, w, 16:], pw[:, w, 16 - (1 << w):16 + SEQ - (1 << w)],
                                               ALU.add))
                    total = pw[:, bass.ds(b + 1, 1), :].rearrange("p a t -> p (a t)")
                    link(dve.scalar_tensor_tensor(ccb[:, :], total[:, 16:], vt[:, bass.ds(b + C_WIN, 1)], pw[:, 0, 16:],
                                                  ALU.mult, ALU.subtract))
                    link(dve.tensor_tensor(pfirst[:, :], total[:, 16:32], vt[:, bass.ds(b * 16 + C_CNT, 16)], ALU.mult))
                    dve.tensor_tensor(ccb[:, 0:16], pfirst[:, :], pw[:, 0, 16:32], ALU.subtract).then_inc(pooled, 1)
                    split(l, 10, b)
                    dve.wait_ge(pooled_hi, s1 + 1)
                    dve.tensor_tensor(pl[:, :], ccb[:, :], ph[:, :].bitcast(f32), ALU.subtract).then_inc(pooled_lo, 1)
                    dve.wait_ge(pv_ready, s1 + 1)
                    dve.tensor_copy(BR[:, 0, bass.ds(b, 1), :].rearrange("p a t -> p (a t)"), bank[3][:, :])\
                       .then_inc(pv_taken, 1)
                    dve.wait_ge(tile_done, n0 + 8)
                    dve.tensor_scalar(BR[:, 2, bass.ds(b, 1), :].rearrange("p a t -> p (a t)"), bank[1][:, :],
                                      vt[:, bass.ds(l * GROUPS + b + C_PS, 1)], None, ALU.mult).then_inc(dve_evac, 1)
                    split(l, 11, b)
                with dve.Fori(0, NB) as j:
                    for m in range(DC):
                        split(l, N_GATE + m + AHEAD, j)
                dve.wait_ge(act_evac, 2 + l * A_ALL + NB * DC)

                def branch_low(j):
                    dve.wait_ge(br_hi, l * NB + j + 1)
                    dve.tensor_tensor(brl[:, j % 2, :, :], BR[:, j, :, :], brh[:, j % 2, :, :].bitcast(f32), ALU.subtract)\
                       .then_inc(br_lo, 1)

                branch_low(0)
                branch_low(1)
                for j in range(NB):
                    for m in range(DC):
                        k = j * (DC // 2) + m // 2
                        if m % 2:
                            dve.wait_ge(tile_done, RING + l * T + N_BR + k + 1)
                        else:
                            dve.wait_ge(half_out, l * (NB * DC // 2) + k + 1)
                        dve.tensor_tensor(G3[:, j, m, :], G3[:, j, m, :], bank[m % 2][:, :], ALU.mult).then_inc(dve_evac, 1)
                        if m % 2:
                            split(l, N_BR + k + AHEAD)
                        if j:
                            dve.wait_ge(dve_evac, 4 + l * V_ALL + V_BR + j * DC + m + 1)
                            add = dve.tensor_tensor(G3[:, 0, m, :], G3[:, 0, m, :], G3[:, j, m, :], ALU.add)
                            if j == 1:
                                link(add)
                            else:
                                add.then_inc(mix_ready, 1)
                                dve.wait_ge(mix_hi, l * DC + m + 1)
                                dve.tensor_tensor(ml[:, m, :], G3[:, 0, m, :], mh[:, m, :].bitcast(f32), ALU.subtract)\
                                   .then_inc(mix_lo, 1)
                    if j == 0:
                        branch_low(2)
                for m in range(DC):
                    dve.wait_ge(tile_done, RING + l * T + N_OUT + m + 1)
                    dve.tensor_tensor(hT[:, m, :], hT[:, m, :], bank[m % 2][:, :], ALU.add).then_inc(dve_evac, 1)
                    split(l, N_OUT + m + AHEAD)
                norm(l, 1)
                dve.wait_ge(keys_hi, l + 1)
                dve.tensor_tensor(keyl[:, :, :], keyraw[:, :, :], keyh[:, :, :].bitcast(f32), ALU.subtract).then_inc(keys_lo, 1)
                with dve.Fori(0, HP // 8) as i:
                    for k in range(8):
                        dve.wait_ge(qh_ready, l * HP + i * 8 + k + 1)
                        dve.tensor_tensor(ql[:, k % 2, :], bank[k % 2][:, :], qh[:, k % 2, :].bitcast(f32), ALU.subtract)\
                           .then_inc(dve_evac, 1)
                        split(l, N_QRY + k + AHEAD, i)
                with steps.loop(NBLK, DVE_TOPK) as c:
                    def batch(n, op):
                        for j in range(n):
                            last = op(j)
                        link(last, True)

                    dve.wait_ge(chunk_ready, l * NBLK + c + 1)
                    apart(dve)

                    def sc(j):
                        return S1[:, j, :]

                    batch(HP, lambda j: dve.max(hv[:, j, 0:8], sc(j)))
                    batch(HP, lambda j: dve.max_index(hx[:, j, 0:8], hv[:, j, 0:8], sc(j)))
                    batch(HP, lambda j: dve.match_replace(S2[:, j, :], hv[:, j, 0:8], sc(j), LOWEST))
                    batch(HP, lambda j: dve.max(hv[:, j, 8:16], S2[:, j, :]))
                    batch(HP, lambda j: dve.max_index(hx[:, j, 8:16], hv[:, j, 8:16], S2[:, j, :]))
                    link(dve.tensor_copy(hxf[:, :, :], hx[:, :, :]))
                    half = [hv[:, z::2, :] for z in range(2)]
                    full = [P, PH, TOPK, TOPK]
                    link(dve.tensor_tensor(cand[:, :, :, :], half[0].unsqueeze(3).to_broadcast(full),
                                           half[1].unsqueeze(2).to_broadcast(full), ALU.add), True)

                    def cd(j):
                        return cand[:, j, :, :].rearrange("p a b -> p (a b)")

                    batch(PH, lambda j: dve.max(tv[:, j, 0:8], cd(j)))
                    batch(PH, lambda j: dve.max_index(tx[:, j, 0:8], tv[:, j, 0:8], cd(j)))
                    batch(PH, lambda j: dve.match_replace(cand2[:, j, :], tv[:, j, 0:8], cd(j), LOWEST))
                    batch(PH, lambda j: dve.max(tv[:, j, 8:16], cand2[:, j, :]))
                    batch(PH, lambda j: dve.max_index(tx[:, j, 8:16], tv[:, j, 8:16], cand2[:, j, :]))
                    dve.tensor_tensor(ex[:, :, :], tv[:, :, :], tv[:, :, 0:1].to_broadcast([P, PH, TOPK]), ALU.subtract)\
                       .then_inc(top_ready, 1)
                    dve.tensor_scalar(txa[:, 0, :, :], tx[:, :, :], 4, None, ALU.logical_shift_right)
                    link(dve.tensor_scalar(txa[:, 1, :, :], tx[:, :, :], TOPK - 1, None, ALU.bitwise_and))
                    link(dve.tensor_copy(txf[:, :, :, :], txa[:, :, :, :]))
                    for z, eq in ((0, eqi), (1, eqj)):
                        link(dve.tensor_tensor(eq[:, :, :, :], txf[:, z, :, :].unsqueeze(3).to_broadcast(full),
                                               iota[:, 0:TOPK].unsqueeze(1).unsqueeze(1).to_broadcast(full), ALU.is_equal))
                        link(dve.tensor_tensor(eq[:, :, :, :], eq[:, :, :, :],
                                               hxf[:, z::2, :].unsqueeze(2).to_broadcast(full), ALU.mult))
                        link(dve.tensor_reduce(slot3[:, z, :, :], eq[:, :, :, :], AX.X, ALU.add))
                    dve.wait_ge(ex_ready, l * NBLK + c + 1)
                    link(dve.tensor_reduce(ssum[:, 0, :], ex[:, :, :], AX.X, ALU.add))
                    link(dve.reciprocal(ssum[:, 1, :], ssum[:, 0, :]))
                    dve.tensor_tensor(slot3[:, 2, :, :], ex[:, :, :], ssum[:, 1, :].unsqueeze(2).to_broadcast([P, PH, TOPK]),
                                      ALU.mult).then_inc(slots_ready, 1)
                    dve.wait_ge(turned, l * NBLK + c + 1)
                    dve.tensor_copy(tabs[:, :, bass.ds(c * P, P)],
                                    bank[6][:, 0:3 * P].rearrange("p (z t) -> p z t", z=3)).then_inc(tabs_ready, 1)
                dve.wait_ge(tabs_ready, (l + 1) * NBLK)
                apart(dve)
                with dve.Fori(0, QUADS // 2) as i:
                    for u in range(2):
                        dve.wait_ge(hot_used, l * QUADS + i * 2 + u + 1)
                        dve.tensor_tensor(RB[:, u, :, :], iota[:, :].unsqueeze(1).to_broadcast([P, 4, NK]),
                                          tabs[:, 1, bass.ds(i * 8 + u * 4, 4)].unsqueeze(2).to_broadcast([P, 4, NK]),
                                          ALU.is_equal)
                        for q in range(4):
                            t = i * 8 + u * 4 + q
                            last = dve.tensor_scalar(LB[:, u, q, :], iota[:, :], tabs[:, 0, bass.ds(t, 1)],
                                                     tabs[:, 2, bass.ds(t, 1)], ALU.is_equal, ALU.mult)
                        last.then_inc(hot_ready, 1)

                def gated(g, u, k, gelu, first=False):
                    if not first:
                        dve.wait_ge(al_ready, l * NK + g * EG + k - 1)
                    dve.tensor_tensor(af[:, k % 2, :].rearrange("p (b t) -> p b t", t=TB),
                                      gelu.rearrange("p (b t) -> p b t", t=TB),
                                      gb[:, u, :, k * TB:(k + 1) * TB], ALU.mult).then_inc(a_ready, 1)

                def low(g, u, k):
                    dve.wait_ge(ah_ready, l * NK + g * EG + k + 1)
                    dve.tensor_tensor(al[:, u, k, :], af[:, k % 2, :], ah[:, u, k, :].bitcast(f32), ALU.subtract)\
                       .then_inc(al_ready, 1)

                def experts(g, u, turn, a, k0, i=0):
                    dve.wait_ge(gate_in[u], l * (NG * 8) + turn * 16)
                    for k in range(EG):
                        dve.wait_ge(act_evac, 2 + l * A_ALL + a + k + 1)
                        gated(g, u, k, ge[:, k % 2, :])
                        split(l, k0 + k + AHEAD, i)
                        low(g, u, k)

                def early_experts(g, turn, first=False):
                    dve.wait_ge(gate_in[0], l * (NG * 8) + turn * 16)
                    dve.wait_ge(early_in, l * (EARLY * 16) + turn * 16)
                    for k in range(EG):
                        gated(g, 0, k, eb[:, k, :], first and k < 2)
                        if k:
                            low(g, 0, k - 1)
                    low(g, 0, EG - 1)

                def gather(g, k0, i=0):
                    for d in range(DC):
                        if d < DC - 1:
                            dve.wait_ge(v_out, l * VO_ALL + g * (DC - 1) + d + 1)
                        else:
                            dve.wait_ge(tile_done, RING + l * T + i * 8 + k0 + EG)
                        dve.tensor_tensor(hT[:, d, :], hT[:, d, :], bank[d % 4][:, :], ALU.add).then_inc(dve_evac, 1)
                        if d % 2:
                            split(l, k0 + d // 2 + AHEAD, i)

                early_experts(0, 1, True)
                dve.wait_ge(lo_split, RAW + l * T + N_1 + AHEAD)
                apart(dve)
                with dve.Fori(0, TURNS1) as i:
                    experts(i * 4 + 1, 1, i * 2 + 1, i * 8 + A_1, N_1, i * 3)
                    gather(i * 4, N_1 + EG, i * 3)
                    early_experts(i * 4 + 2, i * 2 + 2)
                    gather(i * 4 + 1, N_1 + 2 * EG, i * 3)
                    experts(i * 4 + 3, 1, i * 2 + 2, i * 8 + (A_1 + EG), N_1 + 3 * EG, i * 3)
                    gather(i * 4 + 2, N_1 + 4 * EG, i * 3)
                    early_experts(i * 4 + 4, i * 2 + 3)
                    gather(i * 4 + 3, N_1 + 5 * EG, i * 3)
                with dve.Fori(0, TURNS2) as i:
                    experts(i * 2 + (LAST_E + 1), 1, i + (EARLY), i * 8 + A_2, N_2, i * 2)
                    gather(i * 2 + LAST_E, N_2 + EG, i * 2)
                    experts(i * 2 + (LAST_E + 2), 0, i + (EARLY + 1), i * 8 + (A_2 + EG), N_2 + 2 * EG, i * 2)
                    gather(i * 2 + (LAST_E + 1), N_2 + 3 * EG, i * 2)
                experts(NG - 1, 1, NG // 2, A_PLE - EG, N_VL - 2 * EG)
                gather(NG - 2, N_VL - EG)
                gather(NG - 1, N_VL)
                for m in range(DC):
                    if m < DC - 1:
                        dve.wait_ge(v_out, l * VO_ALL + NG * (DC - 1) + m + 1)
                    else:
                        dve.wait_ge(tile_done, RING + l * T + N_PLE)
                    dve.tensor_copy(pj[:, m, :], bank[m % 2][:, :]).then_inc(dve_evac, 1)
                    if m < EG:
                        split(l, N_PT + m + AHEAD)
                norm(l, 2)
                for m in range(DC):
                    dve.wait_ge(act_evac, 2 + l * A_ALL + A_PLE + m + 1)
                    link(dve.tensor_tensor(pj[:, m, :], pj[:, m, :], ge[:, m % 2, :], ALU.mult))
                    dve.tensor_tensor(hT[:, m, :], hT[:, m, :], pj[:, m, :], ALU.add).then_inc(ple_added, 1)
                    split(l, N_PLE + m + AHEAD)

        @block.tensor
        def _(pe):
            pe.sem_inc(tile_done, RING)
            pe.sem_inc(sq_used, 2)
            pe.sem_inc(hot_used, 2)
            pe.wait_ge(const_ready, 1)

            def three(out_ap, w, mov_h, mov_l, first, last):
                slot, a = w
                for i, (st, mv) in enumerate(((hi, mov_h), (hi, mov_l), (lo, mov_h))):
                    ins = pe.matmul(out_ap, st[slot][:, a:a + P], mv, start=first and i == 0, stop=last and i == 2)
                return ins

            def dense(l, k, out_ap, mov, i=0):
                pe.wait_ge(lo_split, RAW + l * T + i * 8 + k + 1)
                for c in range(DC):
                    ins = three(out_ap, (k % RING, c * P), mov[0][:, c, :], mov[1][:, c, :], c == 0, c == DC - 1)
                ins.then_inc(tile_done, 1)

            def norm(l, k):
                o = l * 3 + k
                for c in range(DC):
                    pe.wait_ge(sq_ready, o * DC + c + 1)
                    pe.matmul(bank[2][:, :], ones[:, :], sq[:, c % 2, :], start=c == 0, stop=c == DC - 1)\
                      .then_inc(sq_used, 1)
                pe.wait_ge(xl_ready, o * DC + DC)
                apart(pe)

            with pe.Fori(0, DEPTH) as l:
                norm(l, 0)
                with pe.Fori(0, PAIRS) as b:
                    s1 = l * PAIRS + b
                    v0 = l * V_ALL + b * 8

                    def mix(k):
                        pe.wait_ge(dve_evac, v0 + k + 3)
                        dense(l, k, bank[k % 2][:, :], (xh, xl), b)

                    def ssq(z):
                        pe.wait_ge(qk_sq, s1 * 2 + z + 1)
                        pe.matmul(bank[2 + z][:, :], headones[:, :], ksq[:, :], start=True, stop=True).then_inc(qk_ssq, 1)

                    def scores(h):
                        r = h * DH
                        for s in reversed(range(NBLK)):
                            pe.matmul(bank[4 + s][:, s * P:SEQ], kb[r:r + DH, s * P:(s + 1) * P], qb[r:r + DH, s * P:SEQ],
                                      start=True, stop=True, skip_group_check=True).then_inc(z_ready, 1)

                    def remain(h):
                        a = s1 * 8 + h * 4
                        for i, s in enumerate(reversed(range(NBLK))):
                            pe.wait_ge(sp_masked, a + i + 1)
                            for j in range(s, NBLK):
                                ins = pe.matmul(bank[4 + s][:, j * P:SEQ], (negtri if j == s else negones)[:, :],
                                                attS[:, j, j * P:SEQ], start=False, stop=True, skip_group_check=True)
                            ins.then_inc(arg_ready, 1)

                    def weigh(h):
                        r = h * DH
                        pe.wait_ge(w_masked, s1 * 8 + h * 4 + 4)
                        for s in range(NBLK):
                            ins = pe.matmul(bank[3][r:r + DH, s * P:SEQ], vb[:, s, r:r + DH], attW[:, s, s * P:SEQ],
                                            start=s == 0, stop=s == NBLK - 1, skip_group_check=True)
                        return ins

                    mix(0)
                    mix(1)
                    ssq(0)
                    mix(2)
                    pe.wait_ge(pv_taken, s1 + 1)
                    ssq(1)
                    pe.wait_ge(dve_evac, v0 + 4 + 2)
                    scores(0)
                    pe.wait_ge(dve_evac, v0 + 4 + 3)
                    for s in range(NBLK):
                        ins = pe.transpose(bank[2][:, s * P:(s + 1) * P], vT[:, s * P:(s + 1) * P], ident[:, :])
                    ins.then_inc(v_turned, 1)
                    mix(3)
                    remain(0)
                    mix(4)
                    pe.wait_ge(v_ready, s1 + 1)
                    weigh(0)
                    scores(1)
                    mix(5)
                    remain(1)
                    mix(6)
                    weigh(1).then_inc(pv_ready, 1)
                    pe.wait_ge(pooled_lo, s1 + 1)
                    pe.wait_ge(dve_evac, v0 + 7 + 3)
                    pe.wait_ge(lo_split, RAW + l * T + b * 8 + 8)
                    three(bank[1][:, :], (7, 0), ph[:, :], pl[:, :], True, True).then_inc(tile_done, 1)
                with pe.Fori(0, NB) as j:
                    for m in range(DC):
                        pe.wait_ge(act_evac, l * A_ALL + j * DC + m + 1)
                        dense(l, N_GATE + m, bank[4 + m % 2][:, :], (xh, xl), j)
                for j in range(NB):
                    pe.wait_ge(br_lo, l * NB + j + 1)
                    for m in range(DC):
                        k = N_BR + j * (DC // 2) + m // 2
                        pe.wait_ge(dve_evac, 4 + l * V_ALL + V_BR + j * DC + m - 1)
                        if m % 2 == 0:
                            pe.wait_ge(lo_split, RAW + l * T + k + 1)
                        for c in range(GROUPS):
                            ins = three(bank[m % 2][:, :], (k % RING, (m % 2 * GROUPS + c) * P), brh[:, j % 2, c, :],
                                        brl[:, j % 2, c, :], c == 0, c == GROUPS - 1)
                        ins.then_inc(tile_done if m % 2 else half_out, 1)
                pe.wait_ge(mix_lo, l * DC + DC)
                for m in range(DC):
                    pe.wait_ge(dve_evac, 4 + l * V_ALL + V_OUT + m - 1)
                    dense(l, N_OUT + m, bank[m % 2][:, :], (mh, ml))
                norm(l, 1)
                pe.wait_ge(keys_lo, l + 1)
                apart(pe)

                def key_scores(i, k):
                    n = i * 8 + k
                    pe.wait_ge(dve_evac, 4 + l * V_ALL + V_QRY + n + 1)
                    if k >= 2:
                        pe.wait_ge(sc_ready, l * HP + n - 1)
                    for c in range(NBLK):
                        o = bank[2 + k % 2][:, c * P:(c + 1) * P]
                        kh, kl = (t[:, bass.ds(n, 1), :].rearrange("p a k -> p (a k)") for t in (keyh, keyl))
                        a, b_ = (t[:, k % 2, c * P:(c + 1) * P] for t in (qh, ql))
                        pe.matmul(o, a, kh, start=True, stop=False)
                        pe.matmul(o, a, kl, start=False, stop=False)
                        ins = pe.matmul(o, b_, kh, start=False, stop=True)
                    ins.then_inc(scores_out, 1)

                with pe.Fori(0, HP // 8) as i:
                    for k in range(8):
                        pe.wait_ge(dve_evac, 4 + l * V_ALL + V_QRY + i * 8 + k - 1)
                        dense(l, N_QRY + k, bank[k % 2][:, :], (xh, xl), i)
                        if k:
                            key_scores(i, k - 1)
                    key_scores(i, 7)

                def experts(a, k0, i=0):
                    for k in range(EG):
                        pe.wait_ge(act_evac, l * A_ALL + a + k + 1)
                        dense(l, k0 + k, bank[4 + k % 2][:, :], (xh, xl), i)

                experts(A_EY, N_EY)
                with pe.Fori(0, NBLK) as c:
                    for z in range(2):
                        experts(c * 8 + (A_EY + EG + z * EG), N_EY + EG + z * EG, c)
                    pe.wait_ge(slots_ready, l * NBLK + c + 1)
                    for z in range(3):
                        ins = pe.transpose(bank[6][:, z * P:(z + 1) * P], slot3[:, z, :, :].rearrange("p h k -> p (h k)"),
                                           ident[:, :])
                    ins.then_inc(turned, 1)
                with pe.Fori(0, QUADS // 2) as i:
                    for u in range(2):
                        n = l * QUADS + i * 2 + u
                        pe.wait_ge(hot_ready, n + 1)
                        pe.wait_ge(staged, n + 1)
                        for q in range(4):
                            ins = pe.matmul(bank[6 + u][:, q * P:(q + 1) * P], RB[:, u, q, :], LB[:, u, q, :],
                                            start=True, stop=True)
                        ins.then_inc(hot_used, 1)

                def values(g, u, k0, i=0):
                    pe.wait_ge(al_ready, l * NK + (g + 1) * EG)
                    pe.wait_ge(lo_split, RAW + l * T + i * 8 + k0 + EG)
                    for d in range(DC):
                        pe.wait_ge(dve_evac, l * V_ALL + V_EXP + g * DC + d + 1)
                        for k in range(EG):
                            ins = three(bank[d % 4][:, :], ((k0 + k) % RING, d * P), ah[:, u, k, :], al[:, u, k, :],
                                        k == 0, k == EG - 1)
                            if d == DC - 1:
                                ins.then_inc(tile_done, 1)
                        if d < DC - 1:
                            ins.then_inc(v_out, 1)

                with pe.Fori(0, TURNS1) as i:
                    experts(i * 8 + A_1, N_1, i * 3)
                    values(i * 4, 0, N_1 + EG, i * 3)
                    values(i * 4 + 1, 1, N_1 + 2 * EG, i * 3)
                    experts(i * 8 + (A_1 + EG), N_1 + 3 * EG, i * 3)
                    values(i * 4 + 2, 0, N_1 + 4 * EG, i * 3)
                    values(i * 4 + 3, 1, N_1 + 5 * EG, i * 3)
                with pe.Fori(0, TURNS2) as i:
                    experts(i * 8 + A_2, N_2, i * 2)
                    values(i * 2 + LAST_E, 0, N_2 + EG, i * 2)
                    experts(i * 8 + (A_2 + EG), N_2 + 2 * EG, i * 2)
                    values(i * 2 + (LAST_E + 1), 1, N_2 + 3 * EG, i * 2)
                experts(A_PLE - EG, N_VL - 2 * EG)
                values(NG - 2, 0, N_VL - EG)
                values(NG - 1, 1, N_VL)
                pe.wait_ge(lo_split, RAW + l * T + N_PLE)
                for m in range(DC):
                    pe.wait_ge(dve_evac, 4 + l * V_ALL + V_PJ + m - 1)
                    for c in range(2):
                        pt, w = (N_PT + c) % RING, (N_PT + 2 + c) % RING
                        ins = three(bank[m % 2][:, :], (w, m * P), hi[pt][:, 0:SEQ], lo[pt][:, 0:SEQ], c == 0, c == 1)
                    if m < DC - 1:
                        ins.then_inc(v_out, 1)
                ins.then_inc(tile_done, 4)
                norm(l, 2)
                for m in range(DC):
                    pe.wait_ge(act_evac, l * A_ALL + A_PLE + m + 1)
                    dense(l, N_PLE + m, bank[4 + m % 2][:, :], (xh, xl))


def _tiles(w):
    k, n = w.shape
    return w.reshape(k // P, P, n // P, P).transpose(2, 1, 0, 3).reshape(n // P, P, -1)


def _stream(a, i):
    import numpy as np

    win = _tiles(a["w_in"][i])
    q, k, v, cb, cc, cu, pu = (win[4 * j:4 * j + 4] for j in range(7))
    pmap = np.zeros((GROUPS, P, 1024), win.dtype)
    pmap[:, :, 0:P] = a["pool_w"][i]
    mix = np.stack([q, k, v, cc, cu, cb, pu, pmap], axis=1).reshape(-1, P, 1024)
    br = a["w_branch"][i].reshape(NB, GROUPS, P, DC // 2, 2, P).transpose(0, 3, 2, 4, 1, 5).reshape(-1, P, 1024)
    u = _tiles(a["expert_u"][i].T).reshape(NG, EG, P, 1024)
    v_ = a["expert_v"][i].reshape(NG, EG, P, 1024)
    ex = [u[g] for g in range(0, LAST_E + 1, 2)]
    for g in range(0, LAST_E, 4):
        ex += [u[g + 1], v_[g], v_[g + 1], u[g + 3], v_[g + 2], v_[g + 3]]
    for g in range(LAST_E, NG - 2, 2):
        ex += [u[g + 1], v_[g], u[g + 2], v_[g + 1]]
    ex += [u[NG - 1], v_[NG - 2], v_[NG - 1]]
    pt = np.zeros((2, P, 1024), win.dtype)
    pt[:, :, 0:SEQ] = a["p"][i, 0].T.reshape(2, P, SEQ)
    pj = a["w_ple_proj"][i].reshape(2, P, 1024)
    return [mix, win[28:], br, _tiles(a["w_out"][i]), _tiles(a["w_query"][i])] + ex + [pt, pj, _tiles(a["w_ple_gate"][i])]


def kernel(**inputs):
    import numpy as np
    import concourse.bacc as bacc
    from concourse.bass_utils import run_bass_kernel_spmd as run

    a = {k: np.asarray(v) for k, v in inputs.items()}
    xT = np.ascontiguousarray(a["x"][0].T.reshape(DC, P, SEQ).transpose(1, 0, 2))
    parts = [t for i in range(DEPTH) for t in _stream(a, i)] + [np.zeros((AHEAD, P, 1024), np.float32)]
    stream = np.concatenate(parts, axis=0)
    keys = np.ascontiguousarray(a["sub_keys"].reshape(DEPTH, HP, NK, P).transpose(0, 3, 1, 2))
    vec = np.zeros((P, NVEC), np.float32)
    gains = np.stack([a["norm_mix"], a["norm_ffn"], a["norm_ple"]], axis=1)
    vec[:, C_GAIN:C_QG] = gains.reshape(-1, P).T
    for z, name in ((C_QG, "q_norm"), (C_KG, "k_norm")):
        vec[:, z:z + DEPTH] = np.concatenate([a[name]] * 2, axis=1).T
    vec[:, C_CW:C_PS] = a["conv_w"].reshape(DEPTH, 3, GROUPS, P).transpose(3, 0, 2, 1).reshape(P, -1)
    vec[:, C_PS:C_WIN] = a["pool_scale"].reshape(-1, P).T
    for g in range(GROUPS):
        size = 2 << g
        vec[:, C_WIN + g] = 1.0 / size
        vec[:, C_CNT + 16 * g:C_CNT + 16 * g + 16] = [1.0 / min(t + 1, size) for t in range(16)]
    vec[:, C_EPS], vec[:, C_QEPS] = EPS, EPS * DH
    ins = {"xT": xT, "stream": stream, "keys": keys, "vec": vec}
    nc = bacc.Bacc("TRN2", target_bir_lowering=False, num_devices=1)
    aps = [nc.dram_tensor(f"in_{k}", v.shape, mybir.dt.from_np(v.dtype), kind="ExternalInput").ap() for k, v in ins.items()]
    out = nc.dram_tensor("out_0", (P, DC, SEQ), mybir.dt.float32, kind="ExternalOutput").ap()
    trunk_kernel(nc, *aps, out)
    r = run(nc, [{f"in_{k}": v for k, v in ins.items()}], core_ids=[0])
    got = r.results[0]["out_0"]
    return np.ascontiguousarray(got.transpose(1, 0, 2).reshape(D, SEQ).T).reshape(1, SEQ, D)
```

```python
import concourse.bass as bass
from concourse import mybir
from contextlib import ExitStack, contextmanager

P = 128
D, SEQ, DEPTH = 1024, 512, 2
DC = D // P
DH, SCALE_ROOT = 64, 8.0
NBLK = SEQ // P
PAIRS = 4
GROUPS = 4
NB = 3
HP, NK, TOPK = 16, 128, 16
PH = HP // 2
SLOTS = PH * TOPK
EPS = 1e-6

RING, RAW, AHEAD = 8, 4, 4
EG = 4
NG = NK // EG
N_MIX = 0
N_GATE = N_MIX + 8 * PAIRS
N_BR = N_GATE + NB * DC
N_OUT = N_BR + NB * DC // 2
N_QRY = N_OUT + DC
EARLY = 15
LAST_E = 2 * (EARLY - 1)
N_EY = N_QRY + HP
SEL_T = EG + 8 * NBLK + EG
N_1 = N_EY + EARLY * EG
TURNS1 = LAST_E // 4
N_2 = N_1 + TURNS1 * 6 * EG
TURNS2 = (NG - LAST_E - 2) // 2
N_VL = N_2 + TURNS2 * 4 * EG + 2 * EG
N_PT = N_VL + EG
N_PLE = N_PT + 4
T = N_PLE + DC
assert T % RING == 0 and N_EY % RING == 4 and N_1 % RING == 0 and NG - LAST_E == 2 * TURNS2 + 2

V_MIX = 0
V_BR = V_MIX + 8 * PAIRS
V_OUT = V_BR + NB * DC
V_QRY = V_OUT + DC
V_EXP = V_QRY + HP
V_PJ = V_EXP + NG * DC
V_ALL = V_PJ + DC
A_EY = NB * DC
A_1 = A_EY + EARLY * EG
A_2 = A_1 + TURNS1 * 2 * EG
A_PLE = A_EY + NK
A_ALL = A_PLE + DC
assert V_EXP % 4 == 0 and V_ALL % 4 == 0

C_GAIN = 0
C_QG = C_GAIN + DEPTH * 3 * DC
C_KG = C_QG + DEPTH
C_CW = C_KG + DEPTH
C_PS = C_CW + DEPTH * GROUPS * 3
C_WIN = C_PS + DEPTH * GROUPS
C_CNT = C_WIN + GROUPS
C_EPS = C_CNT + GROUPS * 16
C_QEPS = C_EPS + 1
NVEC = C_QEPS + 1

TB = 32
NTB = SEQ // TB
QUADS = SEQ // 4
assert TB // 4 == DC and EARLY * EG - SEL_T == NTB + EG


VO_ALL = (NG + 1) * (DC - 1)
DVE_LAYER, DVE_PAIR, DVE_TOPK = 152, 11, 22
LOWEST = -3.0e38


class Steps:

    def __init__(self, eng, sem, passed):
        self.eng, self.sem, self.base, self.k, self.passed = eng, sem, 0, 0, passed

    def link(self, ins, apart=False):
        self.k += 1
        ins.then_inc(self.sem, 1)
        self.eng.wait_ge(self.sem, self.base + self.k)
        if apart:
            self.eng.sem_inc(self.passed, 1)

    @contextmanager
    def loop(self, trips, per):
        base, k = self.base, self.k
        with self.eng.Fori(0, trips) as i:
            self.base, self.k = i * per + (base + k), 0
            yield i
            assert self.k == per, f"steps in this loop: {self.k}"
        self.base, self.k = base, k + trips * per


def trunk_kernel(nc, xT, stream, keys, vec, out):
    f32, f32r, u32 = mybir.dt.float32, mybir.dt.float32r, mybir.dt.uint32
    ALU, ACT, AX = mybir.AluOpType, mybir.ActivationFunctionType, mybir.AxisListType
    gate_table = nc.dram_tensor("gate_table", (NTB, P, NK * TB), f32, kind="Internal").ap()
    early = nc.dram_tensor("early", (P, EARLY * EG, SEQ), f32, kind="Internal").ap()

    top = [16512]

    def area(size):
        top[0] += size
        return top[0] - size

    def sb(name, off, shape, dt=f32):
        return nc.alloc_sbuf_tensor_at(name, shape, dt, offset=off)

    KB = 1024
    o_h, o_c, o_raw, o_ring, o_x = area(16 * KB), area(4 * KB), area(16 * KB), area(64 * KB), area(32 * KB)
    o_r, o_t, o_b = area(32 * KB), area(19 * KB), area(24 * KB)
    assert top[0] <= 229368, top[0]

    hT = sb("hT", o_h, [P, DC, SEQ])
    ident = sb("ident", o_c, [P, P])
    ones = sb("ones", o_c + 512, [P, P])
    headones = sb("headones", o_c + 1024, [P, P])
    negtri = sb("negtri", o_c + 1536, [P, P])
    negones = sb("negones", o_c + 2048, [P, P])
    iota = sb("iota", o_c + 2560, [P, NK])
    vt = sb("vt", o_c + 3072, [P, NVEC])
    raw = [sb(f"raw{i}", o_raw + 4 * KB * i, [P, 1024]) for i in range(RAW)]
    hi = [sb(f"hi{i}", o_ring + 8 * KB * i, [P, 1024], f32r) for i in range(RING)]
    lo = [sb(f"lo{i}", o_ring + 8 * KB * i + 4 * KB, [P, 1024], f32r) for i in range(RING)]
    xh = sb("xh", o_x, [P, DC, SEQ], f32r)
    xl = sb("xl", o_x + 16 * KB, [P, DC, SEQ], f32r)
    brh = sb("brh", o_x, [P, 2, GROUPS, SEQ], f32r)
    brl = sb("brl", o_x + 16 * KB, [P, 2, GROUPS, SEQ], f32r)
    sq = sb("sq", o_t + 39 * KB, [P, 2, SEQ])
    xt = sb("xt", o_t + 4 * KB, [P, 2, SEQ])
    rs = sb("rs", o_t + 8 * KB, [P, SEQ])
    attE = sb("attE", o_r, [P, NBLK, SEQ])
    attS = sb("attS", o_r + 8 * KB, [P, NBLK, SEQ])
    attW = sb("attW", o_r + 16 * KB, [P, NBLK, SEQ])
    qb = sb("qb", o_r + 24 * KB, [P, SEQ])
    kb = sb("kb", o_r + 26 * KB, [P, SEQ])
    vb = sb("vb", o_r + 28 * KB, [P, NBLK, P])
    vT = sb("vT", o_r + 30 * KB, [P, SEQ])
    qrs = sb("qrs", o_t, [P, SEQ])
    ksq = sb("ksq", o_t + 2 * KB, [P, SEQ])
    ccb = sb("ccb", o_t + 4 * KB, [P, SEQ])
    uc = sb("uc", o_t + 6 * KB, [P, 2 + SEQ])
    pw = sb("pw", o_t + 8256, [P, 5, 16 + SEQ])
    pfirst = sb("pfirst", o_t + 8256 + 10560, [P, 16])
    pv = sb("pv", o_t, [P, SEQ])
    ph = sb("ph", o_r + 30 * KB, [P, SEQ], f32r)
    pl = sb("pl", o_t + 2 * KB, [P, SEQ], f32r)
    BR = sb("BR", o_b, [P, NB, GROUPS, SEQ])
    G3 = sb("G3", o_r, [P, NB, DC, SEQ])
    mh = sb("mh", o_r + 16 * KB, [P, DC, SEQ], f32r)
    ml = sb("ml", o_r + 32 * KB, [P, DC, SEQ], f32r)
    keyh = sb("keyh", o_r, [P, HP, NK], f32r)
    keyl = sb("keyl", o_r + 8 * KB, [P, HP, NK], f32r)
    qh = sb("qh", o_r + 16 * KB, [P, 2, SEQ], f32r)
    ql = sb("ql", o_r + 20 * KB, [P, 2, SEQ], f32r)
    keyraw = sb("keyraw", o_r + 24 * KB, [P, HP, NK])
    SC = sb("SC", o_t, [P, NBLK, HP, NK])
    tabs = sb("tabs", o_t + 32 * KB, [P, 3, SEQ])
    S1 = sb("S1", o_r + 24 * KB, [P, HP, NK])
    S2 = sb("S2", o_r, [P, HP, NK])
    eqj = sb("eqj", o_r, [P, PH, TOPK, TOPK])
    cand = sb("cand", o_r + 8 * KB, [P, PH, TOPK, TOPK])
    eqi = sb("eqi", o_r + 8 * KB, [P, PH, TOPK, TOPK])
    cand2 = sb("cand2", o_r, [P, PH, TOPK * TOPK])
    o_s = o_r + 16 * KB
    hv = sb("hv", o_s, [P, HP, TOPK])
    hx = sb("hx", o_s + KB, [P, HP, TOPK], u32)
    hxf = sb("hxf", o_s + 2 * KB, [P, HP, TOPK])
    tv = sb("tv", o_s + 3 * KB, [P, PH, TOPK])
    tx = sb("tx", o_s + 3 * KB + 512, [P, PH, TOPK], u32)
    txa = sb("txa", o_s + 4 * KB, [P, 2, PH, TOPK], u32)
    txf = sb("txf", o_s + 5 * KB, [P, 2, PH, TOPK])
    ex = sb("ex", o_s + 6 * KB, [P, PH, TOPK])
    ssum = sb("ssum", o_t + 38 * KB, [P, 2, PH])
    slot3 = sb("slot3", o_s + 6 * KB + 512, [P, 3, PH, TOPK])
    LB = sb("LB", o_r + 24 * KB, [P, 2, 4, NK])
    RB = sb("RB", o_r + 28 * KB, [P, 2, 4, NK])
    eo = sb("eo", o_t + 39 * KB, [P, 2, SEQ])
    stage = sb("stage", o_t, [P, 2, NK, TB])
    ah = sb("ah", o_r, [P, 2, EG, SEQ], f32r)
    al = sb("al", o_r + 16 * KB, [P, 2, EG, SEQ], f32r)
    gb = sb("gb", o_t, [P, 2, NTB, EG * TB])
    ge = sb("ge", o_t + 16 * KB, [P, 2, SEQ])
    af = sb("af", o_t + 20 * KB, [P, 2, SEQ])
    eb = sb("eb", o_t + 24 * KB, [P, EG, SEQ])
    pj = sb("pj", o_t + 20 * KB, [P, DC, SEQ])

    ctx = ExitStack()
    with ctx:
        bank = [ctx.enter_context(nc.psum_tensor(f"bank{i}", [P, SEQ], f32)) for i in range(8)]

        def sem(name):
            return ctx.enter_context(nc.semaphore(name))

        x_in, vec_in, keys_in, out_done = [sem("x_in0"), sem("x_in1")], sem("vec_in"), sem("keys_in"), sem("out_done")
        raw_in = [sem(f"raw_in{i}") for i in range(RAW)]
        hi_split = sem("hi_split")
        lo_split = sem("lo_split")
        tile_done = sem("tile_done")
        half_out = sem("half_out")
        v_out = sem("v_out")
        dve_evac = sem("dve_evac")
        act_evac = sem("act_evac")
        const_ready = sem("const_ready")
        passed = sem("passed")
        sq_ready, sq_used, root_ready = sem("sq_ready"), sem("sq_used"), sem("root_ready")
        xt_ready, xh_ready, xl_ready = sem("xt_ready"), sem("xh_ready"), sem("xl_ready")
        ple_added = sem("ple_added")
        qk_sq, qk_ssq, qk_root = sem("qk_sq"), sem("qk_ssq"), sem("qk_root")
        v_turned, v_ready = sem("v_turned"), sem("v_ready")
        z_ready, abs_ready, ln_ready, sp_ready = sem("z_ready"), sem("abs_ready"), sem("ln_ready"), sem("sp_ready")
        sp_masked, arg_ready, w_ready, w_masked = sem("sp_masked"), sem("arg_ready"), sem("w_ready"), sem("w_masked")
        pv_ready, pv_taken = sem("pv_ready"), sem("pv_taken")
        pooled, pooled_hi, pooled_lo = sem("pooled"), sem("pooled_hi"), sem("pooled_lo")
        br_hi, br_lo, mix_ready, mix_hi, mix_lo = sem("br_hi"), sem("br_lo"), sem("mix_ready"), sem("mix_hi"), sem("mix_lo")
        keys_hi, keys_lo, qh_ready, scores_out, sc_ready = sem("keys_hi"), sem("keys_lo"), sem("qh_ready"), sem("scores_out"), sem("sc_ready")
        top_ready, ex_ready, slots_ready, turned, tabs_ready = sem("top_ready"), sem("ex_ready"), sem("slots_ready"), sem("turned"), sem("tabs_ready")
        chunk_ready = sem("chunk_ready")
        hot_ready = sem("hot_ready")
        hot_used = sem("hot_used")
        staged = sem("staged")
        table_out = [sem("table_out0"), sem("table_out1")]
        gate_in = [sem("gate_in0"), sem("gate_in1")]
        early_in, early_out = sem("early_in"), [sem("early_out0"), sem("early_out1")]
        a_ready, ah_ready, al_ready = sem("a_ready"), sem("ah_ready"), sem("al_ready")
        exp_ready, dve_step, pool_step = sem("exp_ready"), sem("dve_step"), sem("pool_step")

        block = ctx.enter_context(nc.Block())

        def apart(eng):
            eng.sem_inc(passed, 1)

        def number(l, k, i=0):
            return l * T + i * 8 + k, l * (T // RAW) + i * 2 + k // RAW

        def width(k):
            k = k % T
            return P if k < N_GATE and k % 8 == 7 else SEQ if k in (N_PT, N_PT + 1) else 1024

        @block.sync
        def _(sp):
            with sp.Fori(0, (DEPTH * T + AHEAD) // RAW) as i:
                for r in range(RAW):
                    sp.wait_ge(lo_split, i * RAW + r + 1)
                    sp.dma_start(raw[r][:, :], stream[bass.ds(i * RAW + r, 1), :, :].rearrange("a p n -> (a p) n"))\
                      .then_inc(raw_in[r], 16)
            sp.wait_ge(ple_added, 8 + DEPTH * DC)
            sp.dma_start(out, hT[:, :, :]).then_inc(out_done, 16)
            sp.wait_ge(out_done, 16)

        @block.gpsimd
        def _(pool):
            steps = Steps(pool, pool_step, passed)
            steps.link(pool.memset(ones[:, :], 1.0))
            steps.link(pool.memset(headones[:, :], 0.0))
            steps.link(pool.memset(negones[:, :], -1.0))
            steps.link(pool.iota(iota[:, :], [[1, NK]], base=0, channel_multiplier=0,
                                 allow_small_or_imprecise_dtypes=True))
            for r in (0, DH):
                steps.link(pool.memset(headones[r:r + DH, r:r + DH], 1.0))
            steps.link(pool.affine_select(out=ident[:, :], in_=ones[:, :], compare_op=ALU.is_equal, fill=0.0,
                                          base=0, pattern=[[-1, P]], channel_multiplier=1))
            pool.affine_select(out=negtri[:, :], in_=negones[:, :], compare_op=ALU.is_ge, fill=0.0,
                               base=0, pattern=[[-1, P]], channel_multiplier=1).then_inc(const_ready, 1)

            def keep_later(buf, sb_, done):
                d = buf[:, sb_, sb_ * P:(sb_ + 1) * P]
                pool.affine_select(out=d, in_=d, compare_op=ALU.is_gt, fill=0.0,
                                   base=0, pattern=[[1, P]], channel_multiplier=-1).then_inc(done, 1)

            with pool.Fori(0, DEPTH) as l:
                with pool.Fori(0, 2 * PAIRS) as h:
                    a = l * (8 * PAIRS) + h * 4
                    for i, s in enumerate(reversed(range(NBLK))):
                        pool.wait_ge(sp_ready, a + i + 1)
                        apart(pool)
                        keep_later(attS, s, sp_masked)
                    for i, s in enumerate(reversed(range(NBLK))):
                        pool.wait_ge(w_ready, a + i + 1)
                        apart(pool)
                        keep_later(attW, s, w_masked)
                def split(k, i=0):
                    n = l * T + i * 8 + k
                    pool.wait_ge(hi_split, n + 1)
                    pool.tensor_tensor(lo[k % RING][:, :], raw[k % RAW][:, :], hi[k % RING][:, :].bitcast(f32),
                                       ALU.subtract).then_inc(lo_split, 1)

                pool.wait_ge(lo_split, RAW + l * T + N_EY + AHEAD)
                for k in range(AHEAD):
                    split(N_EY + AHEAD + k)
                with pool.Fori(0, (EARLY * EG - AHEAD) // 8) as c:
                    for k in range(8):
                        split(N_EY + 2 * AHEAD + k, c)

        @block.scalar
        def _(act):
            for z in range(2):
                act.dma_start(hT[:, z * DC // 2:(z + 1) * DC // 2, :], xT[:, z * DC // 2:(z + 1) * DC // 2, :]).then_inc(x_in[z], 16)
            act.dma_start(vt[:, :], vec).then_inc(vec_in, 16)
            act.sem_inc(act_evac, 2)
            act.sem_inc(staged, 2)
            for u in range(2):
                act.sem_inc(table_out[u], 16)

            def split(l, k, i=0):
                n, turn = number(l, k, i)
                w = width(k)
                act.wait_ge(raw_in[k % RAW], turn * 16 + 16)
                act.wait_ge(tile_done, n + 1)
                act.activation(hi[k % RING][:, 0:w], raw[k % RAW][:, 0:w], ACT.Copy).then_inc(hi_split, 1)

            def square(l, k, c):
                if k == 0:
                    act.wait_ge(ple_added, l * DC + c + 1)
                elif k == 1:
                    act.wait_ge(dve_evac, 4 + l * V_ALL + V_OUT + c + 1)
                else:
                    act.wait_ge(dve_evac, 4 + l * V_ALL + V_EXP + (NG - 1) * DC + c + 1)
                act.wait_ge(sq_used, (l * 3 + k) * DC + c + 1)
                act.activation(sq[:, c % 2, :], hT[:, c, :], ACT.Square).then_inc(sq_ready, 1)

            def norm(l, k):
                o = l * 3 + k
                act.wait_ge(sq_used, 2 + o * DC + DC)
                act.activation(rs[:, :], bank[6][:, :], ACT.Sqrt, scale=1.0 / D, bias=vt[:, C_EPS:C_EPS + 1])\
                   .then_inc(root_ready, 1)
                for c in range(DC):
                    act.wait_ge(xt_ready, o * DC + c + 1)
                    act.activation(xh[:, c, :], xt[:, c % 2, :], ACT.Copy).then_inc(xh_ready, 1)

            for z in range(2):
                act.wait_ge(x_in[z], 16)
                for c in range(z * DC // 2, (z + 1) * DC // 2):
                    square(0, 0, c)
                    if z == 0:
                        split(0, c)
            act.wait_ge(vec_in, 16)
            with act.Fori(0, DEPTH) as l:
                norm(l, 0)
                with act.Fori(0, PAIRS) as b:
                    n0 = l * T + b * 8 + RING
                    s2 = l * (2 * PAIRS) + b * 2
                    act.wait_ge(tile_done, n0 + 1)
                    act.activation(ksq[:, :], bank[0][:, :], ACT.Square).then_inc(qk_sq, 1)
                    split(l, 4, b)
                    act.wait_ge(qk_ssq, s2 + 1)
                    act.activation(qrs[:, :], bank[2][:, :], ACT.Sqrt, bias=vt[:, C_QEPS:C_QEPS + 1])\
                       .then_inc(qk_root, 1)
                    act.wait_ge(tile_done, n0 + 2)
                    act.activation(ksq[:, :], bank[1][:, :], ACT.Square).then_inc(qk_sq, 1)
                    split(l, 5, b)
                    act.wait_ge(qk_ssq, s2 + 2)
                    act.activation(ksq[:, :], bank[3][:, :], ACT.Sqrt, scale=1.0 / DH, bias=vt[:, C_EPS:C_EPS + 1])\
                       .then_inc(qk_root, 1)
                    split(l, 6, b)
                    for h in range(2):
                        a = (s2 + h) * 4
                        for i, s in enumerate(reversed(range(NBLK))):
                            act.wait_ge(abs_ready, a + i + 1)
                            act.activation(attE[:, s, s * P:SEQ], attE[:, s, s * P:SEQ], ACT.Exp, scale=-1.0)\
                               .then_inc(exp_ready, 1)
                        for i, s in enumerate(reversed(range(NBLK))):
                            act.wait_ge(exp_ready, a + i + 1)
                            act.activation(attE[:, s, s * P:SEQ], attE[:, s, s * P:SEQ], ACT.Ln, bias=1.0)\
                               .then_inc(ln_ready, 1)
                        split(l, 7 if h == 0 else 9, b)
                        if h:
                            act.wait_ge(pooled, l * PAIRS + b + 1)
                            act.activation(ph[:, :], pv[:, :], ACT.Copy).then_inc(pooled_hi, 1)
                        for i, s in enumerate(reversed(range(NBLK))):
                            act.wait_ge(arg_ready, a + i + 1)
                            act.activation(attW[:, s, s * P:SEQ], bank[4 + s][:, s * P:SEQ], ACT.Exp)\
                               .then_inc(w_ready, 1)
                        split(l, 8 if h == 0 else 10, b)
                    split(l, 11, b)
                act.wait_ge(dve_evac, 4 + l * V_ALL + V_BR)
                apart(act)
                with act.Fori(0, NB) as j:
                    for m in range(DC):
                        act.wait_ge(tile_done, RING + l * T + N_GATE + j * 8 + m + 1)
                        act.activation(G3[:, bass.ds(j, 1), m, :].rearrange("p a t -> p (a t)"), bank[4 + m % 2][:, :],
                                       ACT.Sigmoid).then_inc(act_evac, 1)
                        split(l, N_GATE + m + AHEAD, j)
                for j in range(NB):
                    if j < 2:
                        act.wait_ge(tile_done, RING + l * T + N_BR)
                    else:
                        act.wait_ge(tile_done, RING + l * T + N_BR + DC // 2)
                    for c in range(GROUPS):
                        act.activation(brh[:, j % 2, c, :], BR[:, j, c, :], ACT.Copy).then_inc(br_hi, 1)
                    if j > 0:
                        for k in range(DC // 2):
                            split(l, N_BR + (j - 1) * (DC // 2) + k + AHEAD)
                for m in range(DC):
                    if m % 2 == 0:
                        split(l, N_BR + DC + m // 2 + AHEAD)
                    act.wait_ge(mix_ready, l * DC + m + 1)
                    act.activation(mh[:, m, :], G3[:, 0, m, :], ACT.Copy).then_inc(mix_hi, 1)
                for m in range(DC):
                    split(l, N_OUT + m + AHEAD)
                    square(l, 1, m)
                act.wait_ge(tile_done, RING + l * T + N_QRY)
                act.dma_start(keyraw[:, :, :], keys[bass.ds(l, 1), :, :, :].rearrange("a p h k -> (a p) h k"))\
                   .then_inc(keys_in, 16)
                norm(l, 1)
                act.wait_ge(keys_in, l * 16 + 16)
                act.activation(keyh[:, :, :], keyraw[:, :, :], ACT.Copy).then_inc(keys_hi, 1)

                def take_scores(l, i, k):
                    act.wait_ge(scores_out, l * HP + i * 8 + k + 1)
                    act.activation(SC[:, :, bass.ds(i * 8 + k, 1), :].rearrange("p c a k -> p c (a k)"),
                                   bank[2 + k % 2][:, :].rearrange("p (c k) -> p c k", k=NK), ACT.Copy)\
                       .then_inc(sc_ready, 1)

                with act.Fori(0, HP // 8) as i:
                    for k in range(8):
                        act.wait_ge(tile_done, RING + l * T + N_QRY + i * 8 + k + 1)
                        act.activation(qh[:, k % 2, :], bank[k % 2][:, :], ACT.Copy).then_inc(qh_ready, 1)
                        split(l, N_QRY + k + AHEAD, i)
                        if k:
                            take_scores(l, i, k - 1)
                    take_scores(l, i, 7)
                act.wait_ge(keys_lo, l + 1)
                apart(act)

                def early_gelu(e, k, i=0):
                    act.wait_ge(tile_done, RING + l * T + i * 8 + k + 1)
                    act.activation(eo[:, k % 2, :], bank[4 + k % 2][:, :], ACT.Gelu_apprx_tanh).then_inc(act_evac, 1)
                    split(l, k + AHEAD, i)
                    act.wait_ge(act_evac, 2 + l * A_ALL + A_EY + e + 1)
                    act.dma_start(early[:, bass.ds(e, 1), :].rearrange("p a t -> p (a t)"), eo[:, k % 2, :])\
                       .then_inc(early_out[k % 2], 16)

                def early_flushed(l, e):
                    for u in range(2):
                        act.wait_ge(early_out[u], (l * (EARLY * EG) + e) * 8)

                def load_chunk(c):
                    act.activation(S1[:, :, :], SC[:, bass.ds(c, 1), :, :].rearrange("p a h k -> p (a h) k"), ACT.Copy)\
                       .then_inc(chunk_ready, 1)

                def select_turn(c, last=False):
                    for k in range(12 if last else 8):
                        if k >= 2:
                            act.wait_ge(early_out[k % 2], (l * (EARLY * EG) + c * 8 + EG + (k - k % 2)) * 8)
                        early_gelu(c * 8 + (EG + k), N_EY + EG + k, c)
                        if k == (7 if last else 5):
                            act.wait_ge(top_ready, l * NBLK + c + 1)
                            act.activation(ex[:, :, :], ex[:, :, :], ACT.Exp).then_inc(ex_ready, 1)
                            if not last:
                                load_chunk(c + 1)
                    early_flushed(l, SEL_T if last else c * 8 + (EG + 8))
                    apart(act)

                act.wait_ge(sc_ready, (l + 1) * HP)
                load_chunk(0)
                for k in range(EG):
                    if k == 2:
                        early_flushed(l, 2)
                    early_gelu(0 + k, N_EY + k)
                early_flushed(l, EG)
                apart(act)
                with act.Fori(0, NBLK - 1) as c:
                    select_turn(c)
                select_turn(NBLK - 1, True)
                act.wait_ge(tabs_ready, (l + 1) * NBLK)
                apart(act)
                with act.Fori(0, NTB // 8) as i:
                    for k in range(8):
                        act.wait_ge(table_out[k % 2], l * (NTB * 8) + i * 64 + (k // 2 * 16 + 16))
                        for q in range(TB // 4):
                            act.wait_ge(hot_used, 2 + l * QUADS + i * 64 + k * 8 + q + 1)
                            act.activation(stage[:, k % 2, :, q * 4:q * 4 + 4],
                                           bank[6 + q % 2][:, :].rearrange("p (t k) -> p k t", k=NK), ACT.Copy)\
                               .then_inc(staged, 1)
                        act.wait_ge(staged, 2 + l * QUADS + i * 64 + k * 8 + 8)
                        act.dma_start(gate_table[bass.ds(i * 8 + k, 1), :, :].rearrange("a p n -> (a p) n"),
                                      stage[:, k % 2, :, :].rearrange("p k t -> p (k t)")).then_inc(table_out[k % 2], 16)
                        act.wait_ge(early_out[k % 2], (l * (EARLY * EG) + i * 8 + SEL_T + (k - k % 2)) * 8)
                        early_gelu(i * 8 + (SEL_T + k), N_EY + SEL_T + k, i)
                def late_early(k):
                    act.wait_ge(early_out[k % 2], (l * (EARLY * EG) + SEL_T + NTB + (k - k % 2)) * 8)
                    early_gelu(SEL_T + NTB + k, N_EY + SEL_T + NTB + k)

                def fetch(g, u):
                    act.dma_start(gb[:, u, :, :],
                                  gate_table[:, :, bass.ds(g * (EG * TB), EG * TB)].rearrange("b p n -> p b n"))\
                       .then_inc(gate_in[u], 16)

                def fetch_early(e):
                    act.dma_start(eb[:, :, :], early[:, bass.ds(e * EG, EG), :]).then_inc(early_in, 16)

                def high(g, u, k):
                    act.wait_ge(a_ready, l * NK + g * EG + k + 1)
                    act.activation(ah[:, u, k, :], af[:, k % 2, :], ACT.Copy).then_inc(ah_ready, 1)

                def experts(g, u, k0, i=0):
                    for k in range(EG):
                        split(l, k0 + k + AHEAD, i)
                        act.wait_ge(tile_done, RING + l * T + i * 8 + k0 + k + 1)
                        act.activation(ge[:, k % 2, :], bank[4 + k % 2][:, :], ACT.Gelu_apprx_tanh).then_inc(act_evac, 1)
                        high(g, u, k)

                def value_splits(k0, i=0):
                    for k in range(EG):
                        split(l, k0 + k + AHEAD, i)

                def used(g):
                    act.wait_ge(a_ready, l * NK + (g + 1) * EG)

                late_early(0)
                for u in range(2):
                    act.wait_ge(table_out[u], 16 + (l + 1) * (NTB * 8))
                fetch(0, 0)
                fetch_early(0)
                fetch(1, 1)
                for k in range(1, EG):
                    late_early(k)
                for k in range(EG):
                    high(0, 0, k)
                early_flushed(l, EARLY * EG)
                apart(act)
                with act.Fori(0, TURNS1) as i:
                    used(i * 4)
                    fetch_early(i * 2 + 1)
                    fetch(i * 4 + 2, 0)
                    experts(i * 4 + 1, 1, N_1, i * 3)
                    used(i * 4 + 1)
                    fetch(i * 4 + 3, 1)
                    value_splits(N_1 + EG, i * 3)
                    act.wait_ge(tile_done, RING + l * T + i * 24 + N_1 + 2 * EG)
                    for k in range(EG):
                        high(i * 4 + 2, 0, k)
                    fetch_early(i * 2 + 2)
                    fetch(i * 4 + 4, 0)
                    value_splits(N_1 + 2 * EG, i * 3)
                    experts(i * 4 + 3, 1, N_1 + 3 * EG, i * 3)
                    used(i * 4 + 3)
                    fetch(i * 4 + 5, 1)
                    value_splits(N_1 + 4 * EG, i * 3)
                    act.wait_ge(tile_done, RING + l * T + i * 24 + N_1 + 5 * EG)
                    for k in range(EG):
                        high(i * 4 + 4, 0, k)
                    value_splits(N_1 + 5 * EG, i * 3)
                with act.Fori(0, TURNS2) as i:
                    used(i * 2 + LAST_E)
                    fetch(i * 2 + (LAST_E + 2), 0)
                    experts(i * 2 + (LAST_E + 1), 1, N_2, i * 2)
                    value_splits(N_2 + EG, i * 2)
                    used(i * 2 + (LAST_E + 1))
                    fetch(i * 2 + (LAST_E + 3), 1)
                    experts(i * 2 + (LAST_E + 2), 0, N_2 + 2 * EG, i * 2)
                    value_splits(N_2 + 3 * EG, i * 2)
                experts(NG - 1, 1, N_VL - 2 * EG)
                for k in range(EG):
                    split(l, N_VL - EG + k + AHEAD)
                for k in range(EG):
                    split(l, N_VL + k + AHEAD)
                for c in range(DC):
                    square(l, 2, c)
                for k in range(EG):
                    split(l, N_PT + k + AHEAD)
                norm(l, 2)
                for m in range(DC):
                    act.wait_ge(tile_done, RING + l * T + N_PLE + m + 1)
                    if m >= 2:
                        act.wait_ge(ple_added, DC + l * DC + m - 1)
                    act.activation(ge[:, m % 2, :], bank[4 + m % 2][:, :], ACT.Sigmoid).then_inc(act_evac, 1)
                    split(l, N_PLE + m + AHEAD)
                    square(l + 1, 0, m)

        @block.vector
        def _(dve):
            steps = Steps(dve, dve_step, passed)
            link = steps.link
            dve.sem_inc(lo_split, RAW)
            dve.sem_inc(dve_evac, 4)
            dve.sem_inc(ple_added, DC)
            dve.sem_inc(pv_taken, 1)

            def split(l, k, i=0):
                n, _ = number(l, k, i)
                w = width(k)
                dve.wait_ge(hi_split, n + 1)
                dve.tensor_tensor(lo[k % RING][:, 0:w], raw[k % RAW][:, 0:w],
                                  hi[k % RING][:, 0:w].bitcast(f32), ALU.subtract).then_inc(lo_split, 1)

            def inverse(l, k):
                dve.wait_ge(root_ready, l * 3 + k + 1)
                link(dve.reciprocal(rs[:, :], rs[:, :]))

            def norm(l, k):
                o = l * 3 + k

                def low(c):
                    dve.wait_ge(xh_ready, o * DC + c + 1)
                    dve.tensor_tensor(xl[:, c, :], xt[:, c % 2, :], xh[:, c, :].bitcast(f32), ALU.subtract)\
                       .then_inc(xl_ready, 1)

                for c in range(DC):
                    gain = vt[:, bass.ds(l * (3 * DC) + C_GAIN + k * DC + c, 1)]
                    if c >= 2:
                        dve.wait_ge(xl_ready, o * DC + c - 1)
                    dve.scalar_tensor_tensor(xt[:, c % 2, :], hT[:, c, :], gain, rs[:, :], ALU.mult, ALU.mult)\
                       .then_inc(xt_ready, 1)
                    if c:
                        low(c - 1)
                low(DC - 1)
                dve.wait_ge(xl_ready, o * DC + DC)
                apart(dve)

            dve.wait_ge(vec_in, 16)
            for z in range(2):
                dve.wait_ge(x_in[z], 16)
            dve.wait_ge(const_ready, 1)
            for k in range(AHEAD):
                split(0, k)
            with steps.loop(DEPTH, DVE_LAYER) as l:
                inverse(l, 0)
                norm(l, 0)
                dve.memset(uc[:, 0:2], 0.0)
                link(dve.memset(pw[:, :, 0:16], 0.0), True)
                with steps.loop(PAIRS, DVE_PAIR) as b:
                    n0 = l * T + b * 8 + RING
                    s1 = l * PAIRS + b
                    split(l, 4, b)

                    def taken(n):
                        dve.wait_ge(dve_evac, 4 + l * V_ALL + b * 8 + n)

                    dve.wait_ge(qk_root, s1 * 2 + 1)
                    link(dve.reciprocal(qrs[:, :], qrs[:, :]))
                    dve.scalar_tensor_tensor(qb[:, :], bank[0][:, :], vt[:, bass.ds(l + C_QG, 1)], qrs[:, :],
                                             ALU.mult, ALU.mult).then_inc(dve_evac, 1)
                    split(l, 5, b)
                    dve.wait_ge(tile_done, n0 + 3)
                    dve.tensor_copy(vT[:, :], bank[4][:, :]).then_inc(dve_evac, 1)
                    dve.wait_ge(qk_root, s1 * 2 + 2)
                    link(dve.reciprocal(ksq[:, :], ksq[:, :]))
                    dve.scalar_tensor_tensor(kb[:, :], bank[1][:, :], vt[:, bass.ds(l + C_KG, 1)], ksq[:, :],
                                             ALU.mult, ALU.mult).then_inc(dve_evac, 1)

                    def softplus(h, meanwhile):
                        a = s1 * 8 + h * 4
                        for i, s in enumerate(reversed(range(NBLK))):
                            dve.wait_ge(z_ready, a + i + 1)
                            dve.tensor_scalar(attE[:, s, s * P:SEQ].bitcast(u32), bank[4 + s][:, s * P:SEQ].bitcast(u32),
                                              0x7FFFFFFF, None, ALU.bitwise_and).then_inc(abs_ready, 1)
                        meanwhile()
                        for i, s in enumerate(reversed(range(NBLK))):
                            dve.wait_ge(ln_ready, a + i + 1)
                            dve.scalar_tensor_tensor(attS[:, s, s * P:SEQ], bank[4 + s][:, s * P:SEQ], 0.0,
                                                     attE[:, s, s * P:SEQ], ALU.max, ALU.add).then_inc(sp_ready, 1)

                    def turn_v():
                        dve.wait_ge(v_turned, s1 + 1)
                        dve.tensor_copy(vb[:, :, :].rearrange("p s c -> p (s c)"), bank[2][:, :]).then_inc(v_ready, 1)
                        split(l, 6, b)

                    def pool_tokens():
                        taken(4)
                        for w in range(GROUPS):
                            link(dve.tensor_tensor(pw[:, w + 1, 16:], pw[:, w, 16:], pw[:, w, 16 - (1 << w):16 + SEQ - (1 << w)],
                                                   ALU.add))
                        total = pw[:, bass.ds(b + 1, 1), :].rearrange("p a t -> p (a t)")
                        link(dve.scalar_tensor_tensor(pv[:, :], total[:, 16:], vt[:, bass.ds(b + C_WIN, 1)], pw[:, 0, 16:],
                                                      ALU.mult, ALU.subtract))
                        link(dve.tensor_tensor(pfirst[:, :], total[:, 16:32], vt[:, bass.ds(b * 16 + C_CNT, 16)], ALU.mult))
                        dve.tensor_tensor(pv[:, 0:16], pfirst[:, :], pw[:, 0, 16:32], ALU.subtract).then_inc(pooled, 1)

                    softplus(0, turn_v)
                    dve.wait_ge(tile_done, n0 + 4)
                    dve.tensor_copy(pw[:, 0, 16:], bank[0][:, :]).then_inc(dve_evac, 1)
                    split(l, 7, b)
                    dve.wait_ge(tile_done, n0 + 5)
                    dve.tensor_copy(ccb[:, :], bank[1][:, :]).then_inc(dve_evac, 1)
                    split(l, 8, b)
                    softplus(1, pool_tokens)
                    split(l, 9, b)
                    dve.wait_ge(pooled_hi, s1 + 1)
                    dve.tensor_tensor(pl[:, :], pv[:, :], ph[:, :].bitcast(f32), ALU.subtract).then_inc(pooled_lo, 1)
                    taken(5)
                    dve.wait_ge(tile_done, n0 + 6)
                    dve.tensor_tensor(uc[:, 2:2 + SEQ], bank[0][:, :], ccb[:, :], ALU.mult).then_inc(dve_evac, 1)
                    taken(6)
                    y = BR[:, 1, bass.ds(b, 1), :].rearrange("p a t -> p (a t)")

                    def tap(j):
                        return vt[:, bass.ds(l * (GROUPS * 3) + b * 3 + (C_CW + j), 1)]

                    link(dve.tensor_scalar(y, uc[:, 0:SEQ], tap(0), None, ALU.mult))
                    for j in (1, 2):
                        link(dve.scalar_tensor_tensor(y, uc[:, j:j + SEQ], tap(j), y, ALU.mult, ALU.add))
                    split(l, 10, b)
                    dve.wait_ge(tile_done, n0 + 7)
                    dve.tensor_tensor(y, bank[1][:, :], y, ALU.mult).then_inc(dve_evac, 1)
                    dve.wait_ge(pv_ready, s1 + 1)
                    dve.tensor_copy(BR[:, 0, bass.ds(b, 1), :].rearrange("p a t -> p (a t)"), bank[3][:, :])\
                       .then_inc(pv_taken, 1)
                    dve.wait_ge(tile_done, n0 + 8)
                    dve.tensor_scalar(BR[:, 2, bass.ds(b, 1), :].rearrange("p a t -> p (a t)"), bank[2][:, :],
                                      vt[:, bass.ds(l * GROUPS + b + C_PS, 1)], None, ALU.mult).then_inc(dve_evac, 1)
                    split(l, 11, b)
                with dve.Fori(0, NB) as j:
                    for m in range(DC):
                        split(l, N_GATE + m + AHEAD, j)
                dve.wait_ge(act_evac, 2 + l * A_ALL + NB * DC)

                def branch_low(j):
                    for c in range(GROUPS):
                        dve.wait_ge(br_hi, (l * NB + j) * GROUPS + c + 1)
                        dve.tensor_tensor(brl[:, j % 2, c, :], BR[:, j, c, :], brh[:, j % 2, c, :].bitcast(f32), ALU.subtract)\
                           .then_inc(br_lo, 1)

                def mixed_low(m):
                    dve.wait_ge(mix_hi, l * DC + m + 1)
                    dve.tensor_tensor(ml[:, m, :], G3[:, 0, m, :], mh[:, m, :].bitcast(f32), ALU.subtract).then_inc(mix_lo, 1)

                branch_low(0)
                for j in range(NB):
                    for m in range(DC):
                        k = j * (DC // 2) + m // 2
                        if m % 2:
                            dve.wait_ge(tile_done, RING + l * T + N_BR + k + 1)
                        else:
                            dve.wait_ge(half_out, l * (NB * DC // 2) + k + 1)
                        dve.tensor_tensor(G3[:, j, m, :], G3[:, j, m, :], bank[m % 2][:, :], ALU.mult).then_inc(dve_evac, 1)
                        if m % 2:
                            split(l, N_BR + k + AHEAD)
                        if j == 0 and m == 1:
                            branch_low(1)
                        if j == 0 and m == DC - 1:
                            branch_low(2)
                        if j:
                            dve.wait_ge(dve_evac, 4 + l * V_ALL + V_BR + j * DC + m + 1)
                            add = dve.tensor_tensor(G3[:, 0, m, :], G3[:, 0, m, :], G3[:, j, m, :], ALU.add)
                            if j == 1:
                                link(add)
                            else:
                                add.then_inc(mix_ready, 1)
                                if m:
                                    mixed_low(m - 1)
                mixed_low(DC - 1)
                for m in range(DC):
                    dve.wait_ge(tile_done, RING + l * T + N_OUT + m + 1)
                    dve.tensor_tensor(hT[:, m, :], hT[:, m, :], bank[m % 2][:, :], ALU.add).then_inc(dve_evac, 1)
                    split(l, N_OUT + m + AHEAD)
                inverse(l, 1)
                norm(l, 1)
                dve.wait_ge(keys_hi, l + 1)
                dve.tensor_tensor(keyl[:, :, :], keyraw[:, :, :], keyh[:, :, :].bitcast(f32), ALU.subtract).then_inc(keys_lo, 1)
                with dve.Fori(0, HP // 8) as i:
                    for k in range(8):
                        dve.wait_ge(qh_ready, l * HP + i * 8 + k + 1)
                        dve.tensor_tensor(ql[:, k % 2, :], bank[k % 2][:, :], qh[:, k % 2, :].bitcast(f32), ALU.subtract)\
                           .then_inc(dve_evac, 1)
                        split(l, N_QRY + k + AHEAD, i)
                def take_tabs(c):
                    dve.wait_ge(turned, l * NBLK + c + 1)
                    dve.tensor_copy(tabs[:, :, bass.ds(c * P, P)],
                                    bank[6][:, 0:3 * P].rearrange("p (z t) -> p z t", z=3)).then_inc(tabs_ready, 1)

                def select(c, first=False):
                    def batch(n, op):
                        for j in range(n):
                            last = op(j)
                        link(last, True)

                    dve.wait_ge(chunk_ready, l * NBLK + c + 1)
                    apart(dve)

                    def sc(j):
                        return S1[:, j, :]

                    batch(HP, lambda j: dve.max(hv[:, j, 0:8], sc(j)))
                    batch(HP, lambda j: dve.max_index(hx[:, j, 0:8], hv[:, j, 0:8], sc(j)))
                    batch(HP, lambda j: dve.match_replace(S2[:, j, :], hv[:, j, 0:8], sc(j), LOWEST))
                    batch(HP, lambda j: dve.max(hv[:, j, 8:16], S2[:, j, :]))
                    batch(HP, lambda j: dve.max_index(hx[:, j, 8:16], hv[:, j, 8:16], S2[:, j, :]))
                    link(dve.tensor_copy(hxf[:, :, :], hx[:, :, :]))
                    half = [hv[:, z::2, :] for z in range(2)]
                    full = [P, PH, TOPK, TOPK]
                    link(dve.tensor_tensor(cand[:, :, :, :], half[0].unsqueeze(3).to_broadcast(full),
                                           half[1].unsqueeze(2).to_broadcast(full), ALU.add), True)

                    def cd(j):
                        return cand[:, j, :, :].rearrange("p a b -> p (a b)")

                    batch(PH, lambda j: dve.max(tv[:, j, 0:8], cd(j)))
                    batch(PH, lambda j: dve.max_index(tx[:, j, 0:8], tv[:, j, 0:8], cd(j)))
                    batch(PH, lambda j: dve.match_replace(cand2[:, j, :], tv[:, j, 0:8], cd(j), LOWEST))
                    batch(PH, lambda j: dve.max(tv[:, j, 8:16], cand2[:, j, :]))
                    batch(PH, lambda j: dve.max_index(tx[:, j, 8:16], tv[:, j, 8:16], cand2[:, j, :]))
                    dve.tensor_tensor(ex[:, :, :], tv[:, :, :], tv[:, :, 0:1].to_broadcast([P, PH, TOPK]), ALU.subtract)\
                       .then_inc(top_ready, 1)
                    dve.tensor_scalar(txa[:, 0, :, :], tx[:, :, :], 4, None, ALU.logical_shift_right)
                    link(dve.tensor_scalar(txa[:, 1, :, :], tx[:, :, :], TOPK - 1, None, ALU.bitwise_and))
                    link(dve.tensor_copy(txf[:, :, :, :], txa[:, :, :, :]))
                    if not first:
                        take_tabs(c - 1)
                    for z, eq in ((0, eqi), (1, eqj)):
                        link(dve.tensor_tensor(eq[:, :, :, :], txf[:, z, :, :].unsqueeze(3).to_broadcast(full),
                                               iota[:, 0:TOPK].unsqueeze(1).unsqueeze(1).to_broadcast(full), ALU.is_equal))
                        link(dve.tensor_tensor(eq[:, :, :, :], eq[:, :, :, :],
                                               hxf[:, z::2, :].unsqueeze(2).to_broadcast(full), ALU.mult))
                        link(dve.tensor_reduce(slot3[:, z, :, :], eq[:, :, :, :], AX.X, ALU.add))
                    dve.wait_ge(ex_ready, l * NBLK + c + 1)
                    link(dve.tensor_reduce(ssum[:, 0, :], ex[:, :, :], AX.X, ALU.add))
                    link(dve.reciprocal(ssum[:, 1, :], ssum[:, 0, :]))
                    dve.tensor_tensor(slot3[:, 2, :, :], ex[:, :, :], ssum[:, 1, :].unsqueeze(2).to_broadcast([P, PH, TOPK]),
                                      ALU.mult).then_inc(slots_ready, 1)
                select(0, True)
                with steps.loop(NBLK - 1, DVE_TOPK) as c:
                    select(c + 1)
                take_tabs(NBLK - 1)
                dve.wait_ge(tabs_ready, (l + 1) * NBLK)
                apart(dve)
                with dve.Fori(0, QUADS // 2) as i:
                    for u in range(2):
                        dve.wait_ge(hot_used, l * QUADS + i * 2 + u + 1)
                        dve.tensor_tensor(RB[:, u, :, :], iota[:, :].unsqueeze(1).to_broadcast([P, 4, NK]),
                                          tabs[:, 1, bass.ds(i * 8 + u * 4, 4)].unsqueeze(2).to_broadcast([P, 4, NK]),
                                          ALU.is_equal)
                        for q in range(4):
                            t = i * 8 + u * 4 + q
                            last = dve.tensor_scalar(LB[:, u, q, :], iota[:, :], tabs[:, 0, bass.ds(t, 1)],
                                                     tabs[:, 2, bass.ds(t, 1)], ALU.is_equal, ALU.mult)
                        last.then_inc(hot_ready, 1)

                def gated(g, u, k, gelu, first=False):
                    if not first:
                        dve.wait_ge(al_ready, l * NK + g * EG + k - 1)
                    dve.tensor_tensor(af[:, k % 2, :].rearrange("p (b t) -> p b t", t=TB),
                                      gelu.rearrange("p (b t) -> p b t", t=TB),
                                      gb[:, u, :, k * TB:(k + 1) * TB], ALU.mult).then_inc(a_ready, 1)

                def low(g, u, k):
                    dve.wait_ge(ah_ready, l * NK + g * EG + k + 1)
                    dve.tensor_tensor(al[:, u, k, :], af[:, k % 2, :], ah[:, u, k, :].bitcast(f32), ALU.subtract)\
                       .then_inc(al_ready, 1)

                def experts(g, u, turn, a, k0, i=0):
                    for k in range(EG):
                        split(l, k0 + k + AHEAD, i)
                        if k == 0:
                            dve.wait_ge(gate_in[u], l * (NG * 8) + turn * 16)
                        dve.wait_ge(act_evac, 2 + l * A_ALL + a + k + 1)
                        gated(g, u, k, ge[:, k % 2, :])
                        low(g, u, k)

                def early_experts(g, turn, first=False):
                    dve.wait_ge(gate_in[0], l * (NG * 8) + turn * 16)
                    dve.wait_ge(early_in, l * (EARLY * 16) + turn * 16)
                    for k in range(EG):
                        gated(g, 0, k, eb[:, k, :], first and k < 2)
                        if k:
                            low(g, 0, k - 1)
                    low(g, 0, EG - 1)

                def gather(g, k0, i=0):
                    for d in range(DC):
                        if d < DC - 1:
                            dve.wait_ge(v_out, l * VO_ALL + g * (DC - 1) + d + 1)
                        else:
                            dve.wait_ge(tile_done, RING + l * T + i * 8 + k0 + EG)
                        dve.tensor_tensor(hT[:, d, :], hT[:, d, :], bank[d % 4][:, :], ALU.add).then_inc(dve_evac, 1)
                        if d % 2 == 0:
                            split(l, k0 + d // 2 + AHEAD, i)

                early_experts(0, 1, True)
                dve.wait_ge(lo_split, RAW + l * T + N_1 + AHEAD)
                apart(dve)
                with dve.Fori(0, TURNS1) as i:
                    experts(i * 4 + 1, 1, i * 2 + 1, i * 8 + A_1, N_1, i * 3)
                    gather(i * 4, N_1 + EG, i * 3)
                    early_experts(i * 4 + 2, i * 2 + 2)
                    gather(i * 4 + 1, N_1 + 2 * EG, i * 3)
                    experts(i * 4 + 3, 1, i * 2 + 2, i * 8 + (A_1 + EG), N_1 + 3 * EG, i * 3)
                    gather(i * 4 + 2, N_1 + 4 * EG, i * 3)
                    early_experts(i * 4 + 4, i * 2 + 3)
                    gather(i * 4 + 3, N_1 + 5 * EG, i * 3)
                with dve.Fori(0, TURNS2) as i:
                    experts(i * 2 + (LAST_E + 1), 1, i + (EARLY), i * 8 + A_2, N_2, i * 2)
                    gather(i * 2 + LAST_E, N_2 + EG, i * 2)
                    experts(i * 2 + (LAST_E + 2), 0, i + (EARLY + 1), i * 8 + (A_2 + EG), N_2 + 2 * EG, i * 2)
                    gather(i * 2 + (LAST_E + 1), N_2 + 3 * EG, i * 2)
                experts(NG - 1, 1, NG // 2, A_PLE - EG, N_VL - 2 * EG)
                gather(NG - 2, N_VL - EG)
                gather(NG - 1, N_VL)
                for m in range(DC):
                    if m < DC - 1:
                        dve.wait_ge(v_out, l * VO_ALL + NG * (DC - 1) + m + 1)
                    else:
                        dve.wait_ge(tile_done, RING + l * T + N_PLE)
                    dve.tensor_copy(pj[:, m, :], bank[m % 2][:, :]).then_inc(dve_evac, 1)
                    if m < EG:
                        split(l, N_PT + m + AHEAD)
                    if m == EG:
                        inverse(l, 2)
                norm(l, 2)
                for m in range(DC):
                    dve.wait_ge(act_evac, 2 + l * A_ALL + A_PLE + m + 1)
                    link(dve.tensor_tensor(pj[:, m, :], pj[:, m, :], ge[:, m % 2, :], ALU.mult))
                    dve.tensor_tensor(hT[:, m, :], hT[:, m, :], pj[:, m, :], ALU.add).then_inc(ple_added, 1)
                    split(l, N_PLE + m + AHEAD)

        @block.tensor
        def _(pe):
            pe.sem_inc(tile_done, RING)
            pe.sem_inc(sq_used, 2)
            pe.sem_inc(hot_used, 2)
            pe.wait_ge(const_ready, 1)

            def three(out_ap, w, mov_h, mov_l, first, last):
                slot, a = w
                for i, (st, mv) in enumerate(((hi, mov_h), (hi, mov_l), (lo, mov_h))):
                    ins = pe.matmul(out_ap, st[slot][:, a:a + P], mv, start=first and i == 0, stop=last and i == 2)
                return ins

            def dense(l, k, out_ap, mov, i=0, after=None, half=None):
                if half != 1:
                    pe.wait_ge(lo_split, RAW + l * T + i * 8 + k + 1)
                for c in range(DC) if half is None else range(half * DC // 2, (half + 1) * DC // 2):
                    if after is not None:
                        pe.wait_ge(after[0], after[1] + c + 1)
                    ins = three(out_ap, (k % RING, c * P), mov[0][:, c, :], mov[1][:, c, :], c == 0, c == DC - 1)
                if half != 0:
                    ins.then_inc(tile_done, 1)

            def norm_sum(l, k, c):
                pe.wait_ge(sq_ready, (l * 3 + k) * DC + c + 1)
                pe.matmul(bank[6][:, :], ones[:, :], sq[:, c % 2, :], start=c == 0, stop=c == DC - 1,
                          skip_group_check=True).then_inc(sq_used, 1)

            for c in range(DC):
                norm_sum(0, 0, c)
            with pe.Fori(0, DEPTH) as l:
                with pe.Fori(0, PAIRS) as b:
                    s1 = l * PAIRS + b
                    v0 = l * V_ALL + b * 8

                    def taken(n):
                        pe.wait_ge(dve_evac, v0 + 4 + n)

                    def mix(k, to, half=None):
                        dense(l, k, bank[to][:, :], (xh, xl), b, (xl_ready, l * 3 * DC) if k == 0 else None, half)

                    def ssq(z):
                        pe.wait_ge(qk_sq, s1 * 2 + z + 1)
                        pe.matmul(bank[2 + z][:, :], headones[:, :], ksq[:, :], start=True, stop=True).then_inc(qk_ssq, 1)

                    def scores(h):
                        r = h * DH
                        for s in reversed(range(NBLK)):
                            pe.matmul(bank[4 + s][:, s * P:SEQ], kb[r:r + DH, s * P:(s + 1) * P], qb[r:r + DH, s * P:SEQ],
                                      start=True, stop=True, skip_group_check=True).then_inc(z_ready, 1)

                    def remain(h):
                        a = s1 * 8 + h * 4
                        for i, s in enumerate(reversed(range(NBLK))):
                            pe.wait_ge(sp_masked, a + i + 1)
                            for j in range(s, NBLK):
                                ins = pe.matmul(bank[4 + s][:, j * P:SEQ], (negtri if j == s else negones)[:, :],
                                                attS[:, j, j * P:SEQ], start=False, stop=True, skip_group_check=True)
                            ins.then_inc(arg_ready, 1)

                    def weigh(h):
                        r = h * DH
                        pe.wait_ge(w_masked, s1 * 8 + h * 4 + 4)
                        for s in range(NBLK):
                            ins = pe.matmul(bank[3][r:r + DH, s * P:SEQ], vb[:, s, r:r + DH], attW[:, s, s * P:SEQ],
                                            start=s == 0, stop=s == NBLK - 1, skip_group_check=True)
                        return ins

                    taken(-1)
                    mix(0, 0)
                    taken(0)
                    mix(1, 1)
                    ssq(0)
                    mix(2, 4, 0)
                    pe.wait_ge(pv_taken, s1 + 1)
                    ssq(1)
                    mix(2, 4, 1)
                    taken(1)
                    mix(3, 0)
                    taken(3)
                    scores(0)
                    for s in range(NBLK):
                        ins = pe.transpose(bank[2][:, s * P:(s + 1) * P], vT[:, s * P:(s + 1) * P], ident[:, :])
                    ins.then_inc(v_turned, 1)
                    mix(4, 1)
                    remain(0)
                    taken(4)
                    mix(5, 0, 0)
                    pe.wait_ge(v_ready, s1 + 1)
                    weigh(0)
                    scores(1)
                    mix(5, 0, 1)
                    taken(5)
                    mix(6, 1, 0)
                    remain(1)
                    mix(6, 1, 1)
                    pe.wait_ge(pooled_lo, s1 + 1)
                    pe.wait_ge(lo_split, RAW + l * T + b * 8 + 8)
                    three(bank[2][:, :], (7, 0), ph[:, :], pl[:, :], True, True).then_inc(tile_done, 1)
                    weigh(1).then_inc(pv_ready, 1)
                with pe.Fori(0, NB) as j:
                    for m in range(DC):
                        pe.wait_ge(act_evac, l * A_ALL + j * DC + m + 1)
                        dense(l, N_GATE + m, bank[4 + m % 2][:, :], (xh, xl), j)
                for j in range(NB):
                    for m in range(DC):
                        k = N_BR + j * (DC // 2) + m // 2
                        pe.wait_ge(dve_evac, 4 + l * V_ALL + V_BR + j * DC + m - 1)
                        if m % 2 == 0:
                            pe.wait_ge(lo_split, RAW + l * T + k + 1)
                        for c in range(GROUPS):
                            if m == 0:
                                pe.wait_ge(br_lo, (l * NB + j) * GROUPS + c + 1)
                            ins = three(bank[m % 2][:, :], (k % RING, (m % 2 * GROUPS + c) * P), brh[:, j % 2, c, :],
                                        brl[:, j % 2, c, :], c == 0, c == GROUPS - 1)
                        ins.then_inc(tile_done if m % 2 else half_out, 1)
                for m in range(DC):
                    pe.wait_ge(dve_evac, 4 + l * V_ALL + V_OUT + m - 1)
                    dense(l, N_OUT + m, bank[m % 2][:, :], (mh, ml), after=(mix_lo, l * DC) if m == 0 else None)
                    if m:
                        norm_sum(l, 1, m - 1)
                norm_sum(l, 1, DC - 1)

                def key_scores(i, k):
                    n = i * 8 + k
                    pe.wait_ge(dve_evac, 4 + l * V_ALL + V_QRY + n + 1)
                    if k >= 2:
                        pe.wait_ge(sc_ready, l * HP + n - 1)
                    pe.wait_ge(keys_lo, l + 1)
                    for c in range(NBLK):
                        o = bank[2 + k % 2][:, c * P:(c + 1) * P]
                        kh, kl = (t[:, bass.ds(n, 1), :].rearrange("p a k -> p (a k)") for t in (keyh, keyl))
                        a, b_ = (t[:, k % 2, c * P:(c + 1) * P] for t in (qh, ql))
                        pe.matmul(o, a, kh, start=True, stop=False)
                        pe.matmul(o, a, kl, start=False, stop=False)
                        ins = pe.matmul(o, b_, kh, start=False, stop=True)
                    ins.then_inc(scores_out, 1)

                with pe.Fori(0, HP // 8) as i:
                    for k in range(8):
                        pe.wait_ge(dve_evac, 4 + l * V_ALL + V_QRY + i * 8 + k - 1)
                        dense(l, N_QRY + k, bank[k % 2][:, :], (xh, xl), i, (xl_ready, (l * 3 + 1) * DC) if k == 0 else None)
                        if k:
                            key_scores(i, k - 1)
                    key_scores(i, 7)

                def experts(a, k0, i=0):
                    for k in range(EG):
                        pe.wait_ge(act_evac, l * A_ALL + a + k + 1)
                        dense(l, k0 + k, bank[4 + k % 2][:, :], (xh, xl), i)

                experts(A_EY, N_EY)
                def beside(c, z):
                    experts(c * 8 + (A_EY + EG + z * EG), N_EY + EG + z * EG, c)

                def turn_slots(c):
                    pe.wait_ge(slots_ready, l * NBLK + c + 1)
                    for z in range(3):
                        ins = pe.transpose(bank[6][:, z * P:(z + 1) * P], slot3[:, z, :, :].rearrange("p h k -> p (h k)"),
                                           ident[:, :])
                    ins.then_inc(turned, 1)

                beside(0, 0)
                beside(0, 1)
                with pe.Fori(0, NBLK - 1) as c:
                    beside(c + 1, 0)
                    turn_slots(c)
                    beside(c + 1, 1)
                beside(NBLK - 1, 2)
                turn_slots(NBLK - 1)
                with pe.Fori(0, NTB // 8) as i:
                    for k in range(8):
                        pe.wait_ge(act_evac, l * A_ALL + A_EY + SEL_T + i * 8 + k + 1)
                        pe.wait_ge(lo_split, RAW + l * T + i * 8 + N_EY + SEL_T + k + 1)
                        for c in range(DC):
                            n = l * QUADS + i * 64 + (k * 8 + c)
                            pe.wait_ge(hot_ready, n + 1)
                            pe.wait_ge(staged, n + 1)
                            for q in range(4):
                                ins = pe.matmul(bank[6 + c % 2][:, q * P:(q + 1) * P], RB[:, c % 2, q, :], LB[:, c % 2, q, :],
                                                start=True, stop=True)
                            ins.then_inc(hot_used, 1)
                            ins = three(bank[4 + k % 2][:, :], ((N_EY + SEL_T + k) % RING, c * P), xh[:, c, :], xl[:, c, :],
                                        c == 0, c == DC - 1)
                        ins.then_inc(tile_done, 1)

                experts(A_EY + SEL_T + NTB, N_EY + SEL_T + NTB)

                def values(g, u, k0, i=0, summing=False):
                    pe.wait_ge(al_ready, l * NK + (g + 1) * EG)
                    for d in range(DC):
                        pe.wait_ge(dve_evac, l * V_ALL + V_EXP + g * DC + d + 1)
                        for k in range(EG):
                            if d == 0:
                                pe.wait_ge(lo_split, RAW + l * T + i * 8 + k0 + k + 1)
                            ins = three(bank[d % 4][:, :], ((k0 + k) % RING, d * P), ah[:, u, k, :], al[:, u, k, :],
                                        k == 0, k == EG - 1)
                            if d == DC - 1:
                                ins.then_inc(tile_done, 1)
                        if d < DC - 1:
                            ins.then_inc(v_out, 1)
                        if summing and d:
                            norm_sum(l, 2, d - 1)

                with pe.Fori(0, TURNS1) as i:
                    experts(i * 8 + A_1, N_1, i * 3)
                    values(i * 4, 0, N_1 + EG, i * 3)
                    values(i * 4 + 1, 1, N_1 + 2 * EG, i * 3)
                    experts(i * 8 + (A_1 + EG), N_1 + 3 * EG, i * 3)
                    values(i * 4 + 2, 0, N_1 + 4 * EG, i * 3)
                    values(i * 4 + 3, 1, N_1 + 5 * EG, i * 3)
                with pe.Fori(0, TURNS2) as i:
                    experts(i * 8 + A_2, N_2, i * 2)
                    values(i * 2 + LAST_E, 0, N_2 + EG, i * 2)
                    experts(i * 8 + (A_2 + EG), N_2 + 2 * EG, i * 2)
                    values(i * 2 + (LAST_E + 1), 1, N_2 + 3 * EG, i * 2)
                experts(A_PLE - EG, N_VL - 2 * EG)
                values(NG - 2, 0, N_VL - EG)
                values(NG - 1, 1, N_VL, summing=True)
                pe.wait_ge(lo_split, RAW + l * T + N_PLE)
                for m in range(DC):
                    pe.wait_ge(dve_evac, 4 + l * V_ALL + V_PJ + m - 1)
                    for c in range(2):
                        pt, w = (N_PT + c) % RING, (N_PT + 2 + c) % RING
                        ins = three(bank[m % 2][:, :], (w, m * P), hi[pt][:, 0:SEQ], lo[pt][:, 0:SEQ], c == 0, c == 1)
                    if m < DC - 1:
                        ins.then_inc(v_out, 1)
                    if m == 0:
                        norm_sum(l, 2, DC - 1)
                ins.then_inc(tile_done, 4)
                for m in range(DC):
                    pe.wait_ge(act_evac, l * A_ALL + A_PLE + m + 1)
                    dense(l, N_PLE + m, bank[4 + m % 2][:, :], (xh, xl), after=(xl_ready, (l * 3 + 2) * DC) if m == 0 else None)
                    if m:
                        norm_sum(l + 1, 0, m - 1)
                norm_sum(l + 1, 0, DC - 1)


def _tiles(w):
    k, n = w.shape
    return w.reshape(k // P, P, n // P, P).transpose(2, 1, 0, 3).reshape(n // P, P, -1)


def _stream(a, i):
    import numpy as np

    win = _tiles(a["w_in"][i])
    q, k, v, cb, cc, cu, pu = (win[4 * j:4 * j + 4] for j in range(7))
    pmap = np.zeros((GROUPS, P, 1024), win.dtype)
    pmap[:, :, 0:P] = a["pool_w"][i]
    mix = np.stack([q, k, v, pu, cc, cu, cb, pmap], axis=1).reshape(-1, P, 1024)
    br = a["w_branch"][i].reshape(NB, GROUPS, P, DC // 2, 2, P).transpose(0, 3, 2, 4, 1, 5).reshape(-1, P, 1024)
    u = _tiles(a["expert_u"][i].T).reshape(NG, EG, P, 1024)
    v_ = a["expert_v"][i].reshape(NG, EG, P, 1024)
    ex = [u[g] for g in range(0, LAST_E + 1, 2)]
    for g in range(0, LAST_E, 4):
        ex += [u[g + 1], v_[g], v_[g + 1], u[g + 3], v_[g + 2], v_[g + 3]]
    for g in range(LAST_E, NG - 2, 2):
        ex += [u[g + 1], v_[g], u[g + 2], v_[g + 1]]
    ex += [u[NG - 1], v_[NG - 2], v_[NG - 1]]
    pt = np.zeros((2, P, 1024), win.dtype)
    pt[:, :, 0:SEQ] = a["p"][i, 0].T.reshape(2, P, SEQ)
    pj = a["w_ple_proj"][i].reshape(2, P, 1024)
    return [mix, win[28:], br, _tiles(a["w_out"][i]), _tiles(a["w_query"][i])] + ex + [pt, pj, _tiles(a["w_ple_gate"][i])]


def kernel(**inputs):
    import numpy as np
    import concourse.bacc as bacc
    from concourse.bass_utils import run_bass_kernel_spmd as run

    a = {k: np.asarray(v) for k, v in inputs.items()}
    xT = np.ascontiguousarray(a["x"][0].T.reshape(DC, P, SEQ).transpose(1, 0, 2))
    parts = [t for i in range(DEPTH) for t in _stream(a, i)] + [np.zeros((AHEAD, P, 1024), np.float32)]
    stream = np.concatenate(parts, axis=0)
    keys = np.ascontiguousarray(a["sub_keys"].reshape(DEPTH, HP, NK, P).transpose(0, 3, 1, 2))
    vec = np.zeros((P, NVEC), np.float32)
    gains = np.stack([a["norm_mix"], a["norm_ffn"], a["norm_ple"]], axis=1)
    vec[:, C_GAIN:C_QG] = gains.reshape(-1, P).T
    for z, name in ((C_QG, "q_norm"), (C_KG, "k_norm")):
        vec[:, z:z + DEPTH] = np.concatenate([a[name]] * 2, axis=1).T
    vec[:, C_CW:C_PS] = a["conv_w"].reshape(DEPTH, 3, GROUPS, P).transpose(3, 0, 2, 1).reshape(P, -1)
    vec[:, C_PS:C_WIN] = a["pool_scale"].reshape(-1, P).T
    for g in range(GROUPS):
        size = 2 << g
        vec[:, C_WIN + g] = 1.0 / size
        vec[:, C_CNT + 16 * g:C_CNT + 16 * g + 16] = [1.0 / min(t + 1, size) for t in range(16)]
    vec[:, C_EPS], vec[:, C_QEPS] = EPS, EPS * DH
    ins = {"xT": xT, "stream": stream, "keys": keys, "vec": vec}
    nc = bacc.Bacc("TRN2", target_bir_lowering=False, num_devices=1)
    aps = [nc.dram_tensor(f"in_{k}", v.shape, mybir.dt.from_np(v.dtype), kind="ExternalInput").ap() for k, v in ins.items()]
    out = nc.dram_tensor("out_0", (P, DC, SEQ), mybir.dt.float32, kind="ExternalOutput").ap()
    trunk_kernel(nc, *aps, out)
    r = run(nc, [{f"in_{k}": v for k, v in ins.items()}], core_ids=[0])
    got = r.results[0]["out_0"]
    return np.ascontiguousarray(got.transpose(1, 0, 2).reshape(D, SEQ).T).reshape(1, SEQ, D)
```
